# Optimizing a Trainium2 kernel written in Bass

```python
import jax
import jax.numpy as jnp
from jax import lax
import numpy as np

D_MODEL = 1024
BATCH = 1
SEQ = 512
DEPTH = 2

HEAD_DIM = 64
BLOCK = 128
SWA_HEADS = D_MODEL // (2 * HEAD_DIM)
SWA_KV_HEADS = SWA_HEADS // 4
SWA_GROUP = SWA_HEADS // SWA_KV_HEADS
WINDOW = 128
RWKV_HEADS = D_MODEL // (2 * HEAD_DIM)
RWKV_DIM = RWKV_HEADS * HEAD_DIM
DECAY_LORA = 64
ICLR_LORA = 64
GATE_LORA = 128
FOX_HEADS = D_MODEL // HEAD_DIM
FOX_DIM = FOX_HEADS * HEAD_DIM
D_FF = 2816
PLE_DIM = 256
N_EVEN = (DEPTH + 1) // 2
N_ODD = DEPTH // 2
NORM_EPS = 1e-6
GN_EPS = 64e-5
L2_EPS = 1e-12

SWA_Q = SWA_HEADS * HEAD_DIM
SWA_KV = SWA_KV_HEADS * HEAD_DIM
SWA_COLS = SWA_Q + 2 * SWA_KV
RWKV_COLS = 3 * RWKV_DIM + DECAY_LORA + ICLR_LORA + GATE_LORA
RWKV_SPLITS = [RWKV_DIM, 2 * RWKV_DIM, 3 * RWKV_DIM,
               3 * RWKV_DIM + DECAY_LORA, 3 * RWKV_DIM + DECAY_LORA + ICLR_LORA]
EVEN_IN = SWA_COLS + RWKV_COLS
EVEN_OUT = SWA_Q + RWKV_DIM
FOX_IN = 3 * FOX_DIM + FOX_HEADS

kernel_name = "hybrid_swa_rwkv7_fox_macaron"

def rms_norm(x, g):
    xf = x.astype(jnp.float32)
    y = xf * lax.rsqrt(jnp.mean(xf * xf, axis=-1, keepdims=True) + NORM_EPS)
    return (y * g.astype(jnp.float32)).astype(x.dtype)

def swiglu(h, w_gu, w_down):
    g, u = jnp.split(h @ w_gu, 2, axis=-1)
    return (jax.nn.silu(g) * u) @ w_down

def alibi_slopes(n):
    return 2.0 ** (-8.0 * jnp.arange(1, n + 1, dtype=jnp.float32) / n)

def sliding_window_attention(q, k, v, sinks):
    b, s = q.shape[:2]
    nb = s // BLOCK
    scale = HEAD_DIM ** -0.5
    qb = q.reshape(b, nb, BLOCK, SWA_KV_HEADS, SWA_GROUP, HEAD_DIM)
    pad = ((0, 0), (BLOCK, 0), (0, 0), (0, 0))
    kp = jnp.pad(k, pad).reshape(b, nb + 1, BLOCK, SWA_KV_HEADS, HEAD_DIM)
    vp = jnp.pad(v, pad).reshape(b, nb + 1, BLOCK, SWA_KV_HEADS, HEAD_DIM)
    kb = jnp.concatenate([kp[:, :-1], kp[:, 1:]], axis=2)
    vb = jnp.concatenate([vp[:, :-1], vp[:, 1:]], axis=2)
    logits = jnp.einsum('bnqhgd,bnkhd->bnhgqk', qb, kb).astype(jnp.float32) * scale
    qi = jnp.arange(BLOCK)[:, None]
    ki = jnp.arange(2 * BLOCK)[None, :]
    dist = qi + BLOCK - ki
    blk = jnp.arange(nb)[:, None, None]
    valid = (dist >= 0) & (dist < WINDOW) & (blk * BLOCK - BLOCK + ki >= 0)
    slopes = alibi_slopes(SWA_HEADS).reshape(SWA_KV_HEADS, SWA_GROUP)
    logits = logits - slopes[:, :, None, None] * dist.astype(jnp.float32)
    logits = jnp.where(valid[None, :, None, None], logits, -jnp.inf)
    sink = sinks.astype(jnp.float32).reshape(SWA_KV_HEADS, SWA_GROUP)[:, :, None]
    m = jnp.maximum(logits.max(axis=-1), sink)
    pr = jnp.exp(logits - m[..., None])
    denom = pr.sum(axis=-1) + jnp.exp(sink - m)
    pr = pr / denom[..., None]
    out = jnp.einsum('bnhgqk,bnkhd->bnqhgd', pr.astype(v.dtype), vb)
    return out.reshape(b, s, SWA_Q)

def rwkv7_time_mix(h, mu, w0, w2, a0, a2, g2, k_k, k_a, r_k, ln_w, ln_b):
    b, s, _ = h.shape
    f32 = jnp.float32
    shifted = jnp.pad(h[:, :-1], ((0, 0), (1, 0), (0, 0)))
    h = h + (shifted - h) * mu
    r, k, v, xw, xa, xg = jnp.split(h, RWKV_SPLITS, axis=-1)
    wlog = -jax.nn.softplus(-(w0 + jnp.tanh(xw) @ w2)) - 0.5
    a = jax.nn.sigmoid(a0 + xa @ a2)
    g = jax.nn.sigmoid(xg) @ g2
    hd = lambda t: t.astype(f32).reshape(b, s, RWKV_HEADS, HEAD_DIM)
    r, k, v, wlog, a = hd(r), hd(k), hd(v), hd(wlog), hd(a)
    kk = k * k_k.astype(f32).reshape(RWKV_HEADS, HEAD_DIM)
    kk = kk / jnp.maximum(jnp.sqrt(jnp.sum(kk * kk, axis=-1, keepdims=True)), L2_EPS)
    k = k * (1.0 + (a - 1.0) * k_a.astype(f32).reshape(RWKV_HEADS, HEAD_DIM))
    decay = jnp.exp(-jnp.exp(wlog))

    def step(state, inp):
        r_t, w_t, k_t, v_t, kk_t, a_t = inp
        s_kk = jnp.einsum('bhij,bhj->bhi', state, kk_t)
        state = (state * w_t[:, :, None, :]
                 - s_kk[..., None] * (kk_t * a_t)[:, :, None, :]
                 + v_t[..., None] * k_t[:, :, None, :])
        return state, jnp.einsum('bhij,bhj->bhi', state, r_t)

    xs = tuple(jnp.moveaxis(t, 1, 0) for t in (r, decay, k, v, kk, a))
    state0 = jnp.zeros((b, RWKV_HEADS, HEAD_DIM, HEAD_DIM), f32)
    _, y = lax.scan(step, state0, xs)
    y = jnp.moveaxis(y, 0, 1)
    mean = jnp.mean(y, axis=-1, keepdims=True)
    var = jnp.mean(jnp.square(y - mean), axis=-1, keepdims=True)
    y = ((y - mean) * lax.rsqrt(var + GN_EPS) * ln_w.astype(f32).reshape(RWKV_HEADS, HEAD_DIM)
         + ln_b.astype(f32).reshape(RWKV_HEADS, HEAD_DIM))
    y = y + jnp.sum(r * k * r_k.astype(f32), axis=-1, keepdims=True) * v
    return (y.reshape(b, s, RWKV_DIM) * g.astype(f32)).astype(h.dtype)

def forgetting_attention(q, k, v, log_f):
    b, s = q.shape[:2]
    nb = s // BLOCK
    scale = HEAD_DIM ** -0.5
    c = jnp.moveaxis(jnp.cumsum(log_f, axis=1), 1, 2)
    key_pos = jnp.arange(s)

    def one_block(n):
        start = n * BLOCK
        qb = lax.dynamic_slice_in_dim(q, start, BLOCK, axis=1)
        cq = lax.dynamic_slice_in_dim(c, start, BLOCK, axis=2)
        logits = (jnp.einsum('bqhd,bkhd->bhqk', qb, k).astype(jnp.float32) * scale
                  + cq[..., None] - c[:, :, None, :])
        qpos = start + jnp.arange(BLOCK)
        logits = jnp.where(key_pos[None, :] <= qpos[:, None], logits, -jnp.inf)
        pr = jax.nn.softmax(logits, axis=-1)
        return jnp.einsum('bhqk,bkhd->bqhd', pr.astype(v.dtype), v)

    out = lax.map(one_block, jnp.arange(nb))
    return jnp.moveaxis(out, 0, 1).reshape(b, s, FOX_DIM)

def setup_inputs(seed: int = 0) -> dict:
    key = jax.random.key(seed)
    k = jax.random.split(key, 30)
    f32 = jnp.float32
    nrm = lambda kk, shape, scale: jax.random.normal(kk, shape, f32) * scale
    gain = lambda kk, shape: 1.0 + 0.05 * jax.random.normal(kk, shape, f32)
    unif = lambda kk, shape, lo, hi: jax.random.uniform(kk, shape, f32, lo, hi)
    return {
        'x': nrm(k[0], (BATCH, SEQ, D_MODEL), 1.0),
        'p': nrm(k[1], (DEPTH, BATCH, SEQ, PLE_DIM), 1.0),
        'ffn1_norm': gain(k[2], (DEPTH, D_MODEL)),
        'ffn1_w_gu': nrm(k[3], (DEPTH, D_MODEL, 2 * D_FF), D_MODEL ** -0.5),
        'ffn1_w_down': nrm(k[4], (DEPTH, D_FF, D_MODEL), D_FF ** -0.5),
        'mix_norm': gain(k[5], (DEPTH, D_MODEL)),
        'ffn2_norm': gain(k[6], (DEPTH, D_MODEL)),
        'ffn2_w_gu': nrm(k[7], (DEPTH, D_MODEL, 2 * D_FF), D_MODEL ** -0.5),
        'ffn2_w_down': nrm(k[8], (DEPTH, D_FF, D_MODEL), D_FF ** -0.5),
        'ple_norm': gain(k[9], (DEPTH, D_MODEL)),
        'ple_w_gate': nrm(k[10], (DEPTH, D_MODEL, D_MODEL), D_MODEL ** -0.5),
        'ple_w_proj': nrm(k[11], (DEPTH, PLE_DIM, D_MODEL), 0.5 * PLE_DIM ** -0.5),
        'even_w_in': nrm(k[12], (N_EVEN, D_MODEL, EVEN_IN), D_MODEL ** -0.5),
        'even_w_out': nrm(k[13], (N_EVEN, EVEN_OUT, D_MODEL), EVEN_OUT ** -0.5),
        'swa_sinks': nrm(k[14], (N_EVEN, SWA_HEADS), 0.5),
        'rwkv_mu': unif(k[15], (N_EVEN, RWKV_COLS), 0.0, 1.0),
        'rwkv_w0': unif(k[16], (N_EVEN, RWKV_DIM), -5.0, -0.5),
        'rwkv_w2': nrm(k[17], (N_EVEN, DECAY_LORA, RWKV_DIM), 0.5 * DECAY_LORA ** -0.5),
        'rwkv_a0': nrm(k[18], (N_EVEN, RWKV_DIM), 0.1),
        'rwkv_a2': nrm(k[19], (N_EVEN, ICLR_LORA, RWKV_DIM), 0.5 * ICLR_LORA ** -0.5),
        'rwkv_g2': nrm(k[20], (N_EVEN, GATE_LORA, RWKV_DIM), GATE_LORA ** -0.5),
        'rwkv_k_k': 0.85 + nrm(k[21], (N_EVEN, RWKV_DIM), 0.05),
        'rwkv_k_a': 1.0 + nrm(k[22], (N_EVEN, RWKV_DIM), 0.05),
        'rwkv_r_k': nrm(k[23], (N_EVEN, RWKV_HEADS, HEAD_DIM), 0.1),
        'rwkv_ln_w': gain(k[24], (N_EVEN, RWKV_DIM)),
        'rwkv_ln_b': nrm(k[25], (N_EVEN, RWKV_DIM), 0.01),
        'fox_w_in': nrm(k[26], (N_ODD, D_MODEL, FOX_IN), D_MODEL ** -0.5),
        'fox_b_f': unif(k[27], (N_ODD, FOX_HEADS), 1.0, 6.0),
        'fox_w_out': nrm(k[28], (N_ODD, FOX_DIM, D_MODEL), FOX_DIM ** -0.5),
        'final_norm': gain(k[29], (D_MODEL,)),
    }

def reference(x, p, ffn1_norm, ffn1_w_gu, ffn1_w_down, mix_norm, ffn2_norm, ffn2_w_gu,
              ffn2_w_down, ple_norm, ple_w_gate, ple_w_proj, even_w_in, even_w_out,
              swa_sinks, rwkv_mu, rwkv_w0, rwkv_w2, rwkv_a0, rwkv_a2, rwkv_g2, rwkv_k_k,
              rwkv_k_a, rwkv_r_k, rwkv_ln_w, rwkv_ln_b, fox_w_in, fox_b_f, fox_w_out,
              final_norm):
    b, s, _ = x.shape
    for i in range(DEPTH):
        j = i // 2
        x = x + 0.5 * swiglu(rms_norm(x, ffn1_norm[i]), ffn1_w_gu[i], ffn1_w_down[i])
        hn = rms_norm(x, mix_norm[i])
        if i % 2 == 0:
            proj = hn @ even_w_in[j]
            qa, ka, va, hb = jnp.split(proj, [SWA_Q, SWA_Q + SWA_KV, SWA_COLS], axis=-1)
            ya = sliding_window_attention(
                qa.reshape(b, s, SWA_HEADS, HEAD_DIM),
                ka.reshape(b, s, SWA_KV_HEADS, HEAD_DIM),
                va.reshape(b, s, SWA_KV_HEADS, HEAD_DIM),
                swa_sinks[j])
            yb = rwkv7_time_mix(hb, rwkv_mu[j], rwkv_w0[j], rwkv_w2[j], rwkv_a0[j], rwkv_a2[j],
                                rwkv_g2[j], rwkv_k_k[j], rwkv_k_a[j], rwkv_r_k[j],
                                rwkv_ln_w[j], rwkv_ln_b[j])
            mixed = jnp.concatenate([ya, yb], axis=-1) @ even_w_out[j]
        else:
            proj = hn @ fox_w_in[j]
            qc, kc, vc, fz = jnp.split(proj, [FOX_DIM, 2 * FOX_DIM, 3 * FOX_DIM], axis=-1)
            log_f = jax.nn.log_sigmoid(fz.astype(jnp.float32) + fox_b_f[j].astype(jnp.float32))
            yc = forgetting_attention(
                qc.reshape(b, s, FOX_HEADS, HEAD_DIM),
                kc.reshape(b, s, FOX_HEADS, HEAD_DIM),
                vc.reshape(b, s, FOX_HEADS, HEAD_DIM),
                log_f)
            mixed = yc @ fox_w_out[j]
        x = x + mixed
        x = x + 0.5 * swiglu(rms_norm(x, ffn2_norm[i]), ffn2_w_gu[i], ffn2_w_down[i])
        gate = jax.nn.sigmoid(rms_norm(x, ple_norm[i]) @ ple_w_gate[i])
        x = x + gate * (p[i] @ ple_w_proj[i])
    return rms_norm(x, final_norm)


_drawn_inputs = setup_inputs


def setup_inputs(seed=0):
    import zlib

    import numpy as np

    out = dict(_drawn_inputs(seed))
    spreads = {}
    factors = {'ple_norm': 29.033,
     'swa_sinks': 3.969,
     'rwkv_w2': 5.012,
     'rwkv_a0': 3.945,
     'rwkv_k_k': 12.282,
     'rwkv_k_a': 2.869,
     'rwkv_ln_w': 3.059,
     'rwkv_ln_b': 8.0,
     'ffn2_norm': 2.943}
    for name, (base, spread) in spreads.items():
        noise = np.random.default_rng([zlib.crc32(name.encode()), seed]).standard_normal(out[name].shape)
        drawn = base * np.exp(spread * noise) if base else spread * noise
        out[name] = jnp.asarray(drawn.astype(out[name].dtype))
    for name, factor in factors.items():
        out[name] = (out[name] * factor).astype(out[name].dtype)
    return out
```

```python
import math
from contextlib import ExitStack

import concourse.bass as bass
from concourse import mybir

F32 = mybir.dt.float32
F32R = mybir.dt.float32r
ALU = mybir.AluOpType
ACT = mybir.ActivationFunctionType
AX = mybir.AxisListType

P = 128
T = 512
DM = 1024
DT = DM // P
FF = 2816
FT = FF // P
HALVES = (12, 10)
PLE = 256
FOX_HEADS = 16
SWA_HEADS = 8
C = 64
NC = T // C
LEVELS = 6
GN_EPS = 64e-5
L2_EPS = 1e-12
KAPPA = math.exp(-0.5)
RP = 4
PAIRS = FOX_HEADS // 2
NB = T // P
MASKED = 1e30
PT = PLE // P
HD = 64
EPS = 1e-6


STAGES = ("ffn1_0", "even_0", "ffn2_0", "ple_0", "ffn1_1", "fox_1", "ffn2_1", "ple_1")

EVEN_SEMAPHORES = """
    hb_zeroed lora_zeroed dist_ready dist_cut dist_masked slope_ready sink_loaded nsink_ready blank_ready
    swa_v_ready swa_vt_ready swa_vt_copied lora_step lora_ready th_ready gate_ready
    swa_qk_done swa_logit_ready swa_max_ready swa_nm_ready swa_exp_ready swa_den_ready swa_rcp_ready
    swa_p_ready swa_pt_ready swa_pt_copied swa_o_done
    lora_loaded masks_filled
    """.split()

RWKV_STEPS = {
    "tensor": "lora kk_summed v_turned rk_summed kq_turned b_turned ab k_turned ak aab f".split()
    + [f"{name}{level}" for level in range(1, 5) for name in ("x", "mx", "m_turned")]
    + "x5 mx5 we gq h yc".split() + [f"z{c}" for c in range(2, 8)] + "yz gn_summed g gn_var".split(),
    "scalar": """kk kk_squared sigmoids kk_norm decay exps chunk_ends v_by_token kq_by_token b_by_token
        k_by_token aab_copied f_copied m_copied1 m_copied2 m_copied3 m_copied4 we_copied h_copied
        yc_copied gn_squared gn_std""".split(),
    "vector": """k_mixed v_mixed kk_clamped lc lcm r_mixed ka k rk kk_rinv kkn kq kka b_scaled rq k_scaled
        bonus ab_masked ak_masked init init_t m0""".split()
    + [f"{name}{level}" for level in range(1, 6) for name in ("x_masked", "m")]
    + ["gq_copied"] + [f"state{c}" for c in range(1, 8)]
    + "y_raw gn_centred y_weighted bonus_gated gn_rinv gn_normed y_done".split(),
    "pool": "weights_staged diff_k diff_v diff_r b_tail k_tail diag".split(),
}


def ds(i, n=1):
    return bass.ds(i, n)


class Jobs:
    FIRST = 2

    def __init__(self):
        self.tiles = []
        self.phases = {}

    def phase(self, name, tiles):
        self.phases[name] = (len(self.tiles) + self.FIRST, len(tiles))
        self.tiles += tiles

    def of(self, n):
        n -= self.FIRST
        return self.tiles[n] if n < len(self.tiles) else 0


def trunk(nc, dram, out, stages=STAGES):
    ctx = ExitStack()
    with ctx:
        def sb(name, shape, dt=F32, stack=ctx):
            return stack.enter_context(nc.sbuf_tensor(name, shape, dt))

        def sem(name):
            return ctx.enter_context(nc.semaphore(name))

        jobs = Jobs()
        norms = {}
        stage_base = {}
        for st in stages:
            stage_base[st] = len(jobs.tiles) + jobs.FIRST
            norms[st] = len(norms)
            if st.startswith("ffn"):
                jobs.phase(st + "up0", [2 * DT] * HALVES[0])
                jobs.phase(st + "down0", [HALVES[0]] * DT)
                jobs.phase(st + "up1", [2 * DT] * HALVES[1])
                jobs.phase(st + "down1", [HALVES[1]] * DT)
            elif st.startswith("ple"):
                jobs.phase(st, [DT + PT] * DT)
            elif st.startswith("even"):
                jobs.phase(st + "in", [2 * DT] * (2 + 2 * RP))
                jobs.phase(st + "out", [DT] * DT)
            elif st.startswith("fox"):
                jobs.phase(st + "in", [DT] + [2 * DT, DT] * PAIRS)
                jobs.phase(st + "out", [DT] * DT)
        norms["final"] = len(norms)
        mixers = {st: k for k, st in enumerate(s for s in stages if s[:3] in ("fox", "eve"))}
        h_base = {}
        gated_base = {}
        h_count = gated_count = 0
        for st in stages:
            h_base[st], gated_base[st] = h_count, gated_count
            h_count += FT if st.startswith("ffn") else 0
            gated_count += FT if st.startswith("ffn") else DT if st.startswith("ple") else 0
        ple_index = {st: k for k, st in enumerate(s for s in stages if s.startswith("ple"))}

        gain_of = {"ffn1": "ffn1_norm", "ffn2": "ffn2_norm", "ple": "ple_norm", "even": "mix_norm",
                   "fox": "mix_norm"}
        vectors = [dram[gain_of[st[:-2]]][int(st[-1])] for st in stages] + [dram["final_norm"]]
        rwkv = {}
        if "even_0" in stages:
            for name in ("mu", "w0", "a0", "k_k", "k_a", "r_k", "ln_w", "ln_b"):
                v = dram["rwkv_" + name][0]
                rwkv[name] = sum(u.shape[0] for u in vectors) // P
                vectors.append(v.rearrange("h d -> (h d)") if name == "r_k" else v)
        VECS = sum(v.shape[0] for v in vectors) // P

        x = sb("x", [P, DT, T])
        rinv = sb("rinv", [P, T])
        rms = sb("rms", [P, T])
        sq = sb("sq", [P, T])
        sq_sum = sb("sq_sum", [P, T])
        act_in = sb("act_in", [P, T])
        act_out = sb("act_out", [P, T])
        other = sb("other", [P, T])
        prod = sb("prod", [P, T])
        vec_rows = sb("vec_rows", [VECS, P])
        vecs = sb("vecs", [P, VECS])
        gains = vecs[:, 0:len(norms) * DT].rearrange("p (n d) -> p n d", d=DT)
        ident = sb("ident", [P, P])
        ones = sb("ones", [P, P])
        eps_col = sb("eps_col", [P, 1])
        offset = [0]

        def at(kib):
            offset[0] = int(kib * 1024)

        def view(name, shape, dt=F32):
            with ExitStack() as s:
                if offset[0]:
                    s.enter_context(nc.sbuf_tensor("ahead_of_" + name, [P, offset[0] // 4], F32))
                t = s.enter_context(nc.sbuf_tensor(name, shape, dt))
            offset[0] += -(-4 * math.prod(shape[1:]) // 32) * 32
            return t

        W, XN, Y, WORK = 0, 48, 80, 112
        at(W)
        w_raw = [view(f"w_raw{s}", [P, 2 * DT, P]) for s in range(2)]
        w_hi = [view(f"w_hi{s}", [P, 2 * DT, P], F32R) for s in range(2)]
        w_lo = [view(f"w_lo{s}", [P, 2 * DT, P], F32R) for s in range(2)]
        at(XN)
        xn_hi = view("xn_hi", [P, DT, T], F32R)
        xn_lo = view("xn_lo", [P, DT, T], F32R)
        at(Y)
        y_hi = view("y_hi", [P, DT, T], F32R)
        y_lo = view("y_lo", [P, DT, T], F32R)
        at(Y)
        emb_rows = view("emb_rows", [P, T // P, PLE])
        emb_hi = view("emb_hi", [P, PT, T], F32R)
        emb_lo = view("emb_lo", [P, PT, T], F32R)
        at(WORK)
        h_hi = view("h_hi", [P, HALVES[0], T], F32R)
        h_lo = view("h_lo", [P, HALVES[0], T], F32R)
        at(WORK)
        rows_in = view("rows_in", [P, T // P, DM])
        rows_out = view("rows_out", [P, T // P, DM])
        scaled = view("scaled", [P, DT, T])
        at(WORK)
        fox_logit = view("fox_logit", [P, 2, NB * (NB + 1) // 2 * P])
        fox_pt = view("fox_pt", [P, 2, NB, T])
        fox_q = view("fox_q", [P, T])
        fox_k = view("fox_k", [P, T])
        fox_v = view("fox_v", [P, T])
        fox_vt = view("fox_vt", [P, NB, P])
        fox_c = view("fox_c", [P, 2, T])
        fox_cm = view("fox_cm", [P, 2, NB, P])
        fox_cum = view("fox_cum", [FOX_HEADS, T])
        fox_cq = view("fox_cq", [P, NB, FOX_HEADS])
        fox_bf = view("fox_bf", [FOX_HEADS, 1])
        causal = view("causal", [P, P])
        fox_nmax = view("fox_nmax", [P, NB, 2])
        fox_sum = view("fox_sum", [P, NB, 2])
        fox_rcp = view("fox_rcp", [P, NB, 2])
        at(WORK)
        hb = view("hb", [P, 3 * RP, T + 1])
        lora_wa = view("lora_wa", [P, T])
        lora_g = view("lora_g", [P, T])
        th = view("th", [P, T])
        gate_in = view("gate_in", [P, T])
        behind_projections = offset[0] / 1024
        lora_in = view("lora_in", [P, 2, T + 1])
        swa_k = [view(f"swa_k{g}", [P, T]) for g in range(2)]
        swa_v = view("swa_v", [P, T])
        swa_vt = view("swa_vt", [P, NB, P])
        swa_logit = view("swa_logit", [P, 2, NB, 2 * P])
        swa_dist = view("swa_dist", [P, 2 * P])
        swa_slope = view("swa_slope", [P, SWA_HEADS])
        swa_sink = view("swa_sink", [P, SWA_HEADS])
        nsink = view("nsink", [P, SWA_HEADS])
        swa_nmax = view("swa_nmax", [P, 2, NB])
        swa_nm = view("swa_nm", [P, 2, NB])
        swa_sum = view("swa_sum", [P, 2, NB])
        swa_esink = view("swa_esink", [P, 2, NB])
        swa_den = view("swa_den", [P, 2, NB])
        swa_rcp = view("swa_rcp", [P, 2, NB])
        constants_at = max(offset[0], int(behind_projections * 1024) + 4 * 6 * T * 2 + 4 * 2 * NC)
        offset[0] = constants_at
        masks = view("masks", [P, 9, C])
        eye = view("eye", [P, C])
        chunk_start = view("chunk_start", [P, T])
        head_ones = view("head_ones", [P, P])
        gn_eps = view("gn_eps", [P, 1])
        at(Y + 8)
        swa_p = view("swa_p", [P, 2, NB, 2 * P])
        swa_q = view("swa_q", [P, RP, T])
        swa_pt = view("swa_pt", [P, 2, NB, 2, P])

        at(XN)
        kf = view("kf", [P, 2, NC, 2, C])
        ba = view("ba", [P, 2, NC, 2, C])
        aw = view("aw", [P, 2, NC, 2, C])
        kr = view("kr", [P, 2, NC, 2, C])
        at(W + 4)
        m_inv = view("m_inv", [P, 2, NC, C])
        at(W + 12)
        x1 = view("x1", [P, 2, NC, C])
        at(behind_projections)
        bk = view("bk", [P, 2, NC, 2, C])
        ktok = view("ktok", [P, 2, NC, C])
        vtok = view("vtok", [P, 2, NC, C])
        ark = view("ark", [P, 2, NC, C])
        mt_inv = view("mt_inv", [P, 2, NC, C])
        chunk_end = view("chunk_end", [P, 2, NC])
        assert offset[0] <= constants_at
        at(Y + 12)
        bonus = view("bonus", [P, 2, T])
        at(Y + 28)
        lora_wa_pair = view("lora_wa_pair", [P, 2, P])
        lora_g_pair = view("lora_g_pair", [P, 2, P])
        tmp = [[act_in, act_out, other, prod, sq, sq_sum, rms, rinv], []]
        for k in range(8):
            at(W + 20 + 8 * (k // 2) + 2 * (k % 2))
            tmp[1].append(view(f"tmp{k}", [P, T]))

        cum_dram = nc.dram_tensor("cum_dram", [FOX_HEADS, T], F32, kind="Internal").ap()

        bank = [ctx.enter_context(nc.psum_tensor(f"bank{b}", [P, T], F32)) for b in range(8)]

        consts_ready = sem("consts_ready")
        rows_loaded = [sem(f"rows_loaded{b}") for b in range(T // P)]
        vecs_t_ready = sem("vecs_t_ready")
        vecs_ready = sem("vecs_ready")
        vecs_loaded = sem("vecs_loaded")
        w_loaded = [sem(f"w_loaded{s}") for s in range(2)]
        w_hi_ready = sem("w_hi_ready")
        w_ready = sem("w_ready")
        job_done = sem("job_done")
        banks_free = sem("banks_free")
        x_ready = sem("x_ready")
        xn_hi_ready = sem("xn_hi_ready")
        xn_ready = sem("xn_ready")
        sq_ready = sem("sq_ready")
        sq_sum_ready = sem("sq_sum_ready")
        ms_ready = sem("ms_ready")
        rms_ready = sem("rms_ready")
        rinv_ready = sem("rinv_ready")
        act_in_ready = sem("act_in_ready")
        act_out_ready = sem("act_out_ready")
        prod_ready = sem("prod_ready")
        h_hi_ready = sem("h_hi_ready")
        h_ready = sem("h_ready")
        xt_ready = sem("xt_ready")
        scaled_ready = sem("scaled_ready")
        ot_ready = sem("ot_ready")
        ot_by_vector = sem("ot_by_vector")
        ot_by_scalar = sem("ot_by_scalar")
        out_stored = sem("out_stored")
        emb_loaded = sem("emb_loaded")
        emb_t_ready = sem("emb_t_ready")
        emb_hi_ready = sem("emb_hi_ready")
        emb_ready = sem("emb_ready")

        y_hi_ready = sem("y_hi_ready")
        y_ready = sem("y_ready")
        causal_ready = sem("causal_ready")
        ones_row_ready = sem("ones_row_ready")
        z_ready = sem("z_ready")
        z_neg_ready = sem("z_neg_ready")
        z_exp_ready = sem("z_exp_ready")
        z_log_ready = sem("z_log_ready")
        log_f_ready = sem("log_f_ready")
        cum_ready = sem("cum_ready")
        cum_stored = sem("cum_stored")
        cq_t_ready = sem("cq_t_ready")
        cq_ready = sem("cq_ready")
        bf_loaded = sem("bf_loaded")
        c_loaded = sem("c_loaded")
        cm_ready = sem("cm_ready")
        v_ready = sem("v_ready")
        vt_ready = sem("vt_ready")
        vt_copied = sem("vt_copied")
        qk_done = sem("qk_done")
        logit_ready = sem("logit_ready")
        max_ready = sem("max_ready")
        exp_ready = sem("exp_ready")
        rcp_ready = sem("rcp_ready")
        p_ready = sem("p_ready")
        pt_ready = sem("pt_ready")
        pt_copied = sem("pt_copied")
        o_done = sem("o_done")
        E = {name: sem(name) for name in EVEN_SEMAPHORES}
        rwkv_waited = sem("rwkv_waited")
        steps_done = {engine: sem(f"rwkv_{engine}_steps") for engine in RWKV_STEPS}

        block = ctx.enter_context(nc.Block())

        def each_job(e, name, step, peel_first=False):
            base, count = jobs.phases[name]
            lead = 2 if peel_first else 0
            for j in range(lead):
                step(base + j, j, (base + j) % 2, jobs.of(base + j + 2))
            if count - 2 > lead:
                with e.Fori(0, (count - 2 - lead) // 2) as i:
                    for s in range(2):
                        step(i * 2 + (base + lead + s), i * 2 + (lead + s), (base + lead + s) % 2,
                             jobs.of(base + lead + s + 2))
            for j in range(count - 2, count):
                step(base + j, j, (base + j) % 2, jobs.of(base + j + 2))

        def loads_due(n, slot):
            return 32 * (n // 2) if isinstance(n, int) else n * 16 - 16 * slot

        def load_tiles(e, n, slot, first, tiles, src):
            e.dma_start(w_raw[slot][:, first:first + tiles], src).then_inc(w_loaded[slot], 16)

        def split_hi(act, n, slot, tiles):
            if tiles:
                act.wait_ge(w_loaded[slot], loads_due(n, slot))
                nc.scalar.copy(w_hi[slot][:, 0:tiles], w_raw[slot][:, 0:tiles]).then_inc(w_hi_ready, 1)

        def split_lo(dve, n, slot, tiles):
            if tiles:
                dve.wait_ge(w_hi_ready, n + 1)
                nc.vector.tensor_tensor(w_lo[slot][:, 0:tiles], w_raw[slot][:, 0:tiles],
                                        w_hi[slot][:, 0:tiles].bitcast(F32),
                                        ALU.subtract).then_inc(w_ready, 1)

        def product(dst, slot, first, tiles, hi, lo, before=None):
            for k in range(tiles):
                if before is not None:
                    before(k)
                w = (w_hi[slot][:, first + k], w_lo[slot][:, first + k])
                nc.tensor.matmul(dst, w[0], hi[:, k], start=k == 0, stop=False)
                nc.tensor.matmul(dst, w[1], hi[:, k], start=False, stop=False)
                last = nc.tensor.matmul(dst, w[0], lo[:, k], start=False, stop=k == tiles - 1)
            return last

        def gain_hi(act, norm, d):
            if norm == norms["final"]:
                act.wait_ge(x_ready, d + (DT * norm + 1))
                nc.scalar.activation(scaled[:, ds(d)], x[:, ds(d)], ACT.Copy,
                                     scale=gains[:, norm, ds(d)]).then_inc(scaled_ready, 1)
                return
            act.wait_ge(x_ready, d + (DT * norm + 1))
            nc.scalar.activation(xn_hi[:, ds(d)], x[:, ds(d)], ACT.Copy,
                                 scale=gains[:, norm, ds(d)]).then_inc(xn_hi_ready, 1)

        def gain_lo(dve, norm, d):
            if norm == norms["final"]:
                return
            dve.wait_ge(xn_hi_ready, d + (DT * norm + 1))
            nc.vector.scalar_tensor_tensor(xn_lo[:, ds(d)], x[:, ds(d)], gains[:, norm, ds(d)],
                                           xn_hi[:, ds(d)].bitcast(F32), ALU.mult,
                                           ALU.subtract).then_inc(xn_ready, 1)

        def square_sum(pool, norm):
            pool.wait_ge(x_ready, DT * norm + 1)
            if norm:
                pool.wait_ge(ms_ready, norm)
            nc.gpsimd.tensor_tensor(sq_sum[:], x[:, 0], x[:, 0], ALU.mult).then_inc(sq_sum_ready, 1)
            with pool.Fori(1, DT) as d:
                pool.wait_ge(x_ready, d + (DT * norm + 1))
                pool.wait_ge(sq_sum_ready, d + DT * norm)
                nc.gpsimd.tensor_tensor(sq[:], x[:, ds(d)], x[:, ds(d)], ALU.mult).then_inc(sq_ready, 1)
                pool.wait_ge(sq_ready, d + (DT - 1) * norm)
                nc.gpsimd.tensor_tensor(sq_sum[:], sq_sum[:], sq[:], ALU.add).then_inc(sq_sum_ready, 1)

        def mean_square(pe, norm):
            pe.wait_ge(sq_sum_ready, DT * (norm + 1))
            if norm:
                pe.wait_ge(rms_ready, norm)
            nc.tensor.matmul(bank[4][:], ones[:], sq_sum[:], start=True, stop=True).then_inc(ms_ready, 1)

        def root(act, norm):
            act.wait_ge(ms_ready, norm + 1)
            if norm:
                act.wait_ge(rinv_ready, norm)
            nc.scalar.activation(rms[:], bank[4][:], ACT.Sqrt, bias=eps_col[:],
                                 scale=1.0 / DM).then_inc(rms_ready, 1)

        def inverse(dve, norm):
            dve.wait_ge(rms_ready, norm + 1)
            nc.vector.reciprocal(rinv[:], rms[:]).then_inc(rinv_ready, 1)

        def ffn_load(e, st, w_gu, w_down):
            gu = w_gu.rearrange("(k p) f -> p k f", p=P)
            f0 = 0
            for half, tiles in enumerate(HALVES):
                def up(n, j, slot, _):
                    e.wait_ge(w_ready, n - 1)
                    for part in range(2):
                        col = j * P + (part * FF + f0 * P)
                        load_tiles(e, n, slot, part * DT, DT, gu[:, :, ds(col, P)])
                each_job(e, f"{st}up{half}", up)
                down_rows = w_down[f0 * P:(f0 + tiles) * P].rearrange("(k p) f -> p k f", p=P)

                def down(n, j, slot, _):
                    e.wait_ge(w_ready, n - 1)
                    for k in (0, tiles // 2):
                        load_tiles(e, n, slot, k, tiles // 2,
                                   down_rows[:, k:k + tiles // 2, ds(j * P, P)])
                each_job(e, f"{st}down{half}", down)
                f0 += tiles

        def ffn_tensor(pe, st):
            norm = norms[st]
            h0 = h_base[st]
            for half, tiles in enumerate(HALVES):
                def up(n, j, slot, _):
                    first = half == 0 and isinstance(j, int) and j == 0
                    pe.wait_ge(w_ready, n + 1)
                    pe.wait_ge(banks_free, n - 1)
                    product(bank[2 * slot][:], slot, 0, DT, xn_hi, xn_lo,
                            (lambda k: pe.wait_ge(xn_ready, DT * norm + k + 1)) if first else None)
                    if first:
                        mean_square(pe, norm)
                    product(bank[2 * slot + 1][:], slot, DT, DT, xn_hi, xn_lo).then_inc(job_done, 1)
                each_job(pe, f"{st}up{half}", up, peel_first=half == 0)

                def down(n, j, slot, _):
                    first = isinstance(j, int) and j == 0
                    pe.wait_ge(w_ready, n + 1)
                    pe.wait_ge(banks_free, n - 1)
                    product(bank[2 * slot][:], slot, 0, tiles, h_hi, h_lo,
                            (lambda k: pe.wait_ge(h_ready, h0 + k + 1)) if first else None
                            ).then_inc(job_done, 1)
                each_job(pe, f"{st}down{half}", down, peel_first=True)
                h0 += tiles

        def ffn_scalar(act, st):
            norm = norms[st]
            root(act, norm)
            h0, g0 = h_base[st], gated_base[st]
            for half, tiles in enumerate(HALVES):
                def up(n, j, slot, ahead):
                    act.wait_ge(job_done, n + 1)
                    split_hi(act, n + 2, slot, ahead)
                    act.wait_ge(act_in_ready, j + (g0 + 1))
                    nc.scalar.activation(act_out[:], act_in[:], ACT.Silu).then_inc(act_out_ready, 1)
                    act.wait_ge(prod_ready, j + (h0 + 1))
                    nc.scalar.copy(h_hi[:, ds(j)], prod[:]).then_inc(h_hi_ready, 1)
                each_job(act, f"{st}up{half}", up)
                g0 += tiles
                h0 += tiles

                def down(n, j, slot, ahead):
                    if half:
                        gain_hi(act, norm + 1, j)
                    act.wait_ge(job_done, n + 1)
                    split_hi(act, n + 2, slot, ahead)
                each_job(act, f"{st}down{half}", down)

        def ffn_vector(dve, st):
            norm = norms[st]
            inverse(dve, norm)
            dve.wait_ge(rinv_ready, norm + 1)
            h0, g0 = h_base[st], gated_base[st]
            for half, tiles in enumerate(HALVES):
                def up(n, j, slot, ahead):
                    dve.wait_ge(job_done, n + 1)
                    nc.vector.tensor_tensor(act_in[:], bank[2 * slot][:], rinv[:],
                                            ALU.mult).then_inc(act_in_ready, 1)
                    nc.vector.tensor_tensor(other[:], bank[2 * slot + 1][:], rinv[:],
                                            ALU.mult).then_inc(banks_free, 1)
                    split_lo(dve, n + 2, slot, ahead)
                    dve.wait_ge(act_out_ready, j + (g0 + 1))
                    dve.wait_ge(banks_free, n + 1)
                    nc.vector.tensor_tensor(prod[:], act_out[:], other[:],
                                            ALU.mult).then_inc(prod_ready, 1)
                    dve.wait_ge(h_hi_ready, j + (h0 + 1))
                    nc.vector.tensor_tensor(h_lo[:, ds(j)], prod[:], h_hi[:, ds(j)].bitcast(F32),
                                            ALU.subtract).then_inc(h_ready, 1)
                each_job(dve, f"{st}up{half}", up)
                g0 += tiles
                h0 += tiles

                def down(n, j, slot, ahead):
                    dve.wait_ge(job_done, n + 1)
                    step = nc.vector.scalar_tensor_tensor(x[:, ds(j)], bank[2 * slot][:], 0.5,
                                                          x[:, ds(j)], ALU.mult, ALU.add)
                    if half:
                        step.then_inc(x_ready, 1)
                        dve.wait_ge(x_ready, j + (DT * (norm + 1) + 1))
                        dve.sem_inc(banks_free, 1)
                        gain_lo(dve, norm + 1, j)
                    else:
                        step.then_inc(banks_free, 1)
                    split_lo(dve, n + 2, slot, ahead)
                each_job(dve, f"{st}down{half}", down)

        def ple_load_rows(e, st, p):
            e.wait_ge(job_done, stage_base[stages[norms[st] - 1]])
            e.dma_start(emb_rows[:], p.rearrange("(b p) c -> p b c", p=P)).then_inc(emb_loaded, 16)

        def ple_load(e, st, w_gate, w_proj):
            gate = w_gate.rearrange("(k p) c -> p k c", p=P)
            proj = w_proj.rearrange("(k p) c -> p k c", p=P)

            def job(n, j, slot, _):
                e.wait_ge(w_ready, n - 1)
                load_tiles(e, n, slot, 0, DT, gate[:, :, ds(j * P, P)])
                load_tiles(e, n, slot, DT, PT, proj[:, :, ds(j * P, P)])
            each_job(e, st, job)

        def ple_tensor(pe, st):
            norm, m = norms[st], ple_index[st]

            def job(n, j, slot, _):
                first = isinstance(j, int) and j == 0
                pe.wait_ge(w_ready, n + 1)
                pe.wait_ge(banks_free, n - 1)
                product(bank[2 * slot][:], slot, 0, DT, xn_hi, xn_lo,
                        (lambda k: pe.wait_ge(xn_ready, DT * norm + k + 1)) if first else None)
                if first:
                    mean_square(pe, norm)
                    pe.wait_ge(emb_loaded, 16 * (m + 1))
                    for k in range(PT):
                        for b in range(T // P):
                            last = nc.tensor.transpose(bank[5 + k][:, b * P:(b + 1) * P],
                                                       emb_rows[:, b, k * P:(k + 1) * P], ident[:])
                        last.then_inc(emb_t_ready, 1)
                    pe.wait_ge(emb_ready, PT * (m + 1))
                product(bank[2 * slot + 1][:], slot, DT, PT, emb_hi, emb_lo).then_inc(job_done, 1)
            each_job(pe, st, job, peel_first=True)

        def ple_scalar(act, st):
            norm, m = norms[st], ple_index[st]
            for k in range(PT):
                act.wait_ge(emb_t_ready, PT * m + k + 1)
                nc.scalar.copy(emb_hi[:, k], bank[5 + k][:]).then_inc(emb_hi_ready, 1)
            root(act, norm)

            def job(n, j, slot, ahead):
                act.wait_ge(job_done, n + 1)
                split_hi(act, n + 2, slot, ahead)
                act.wait_ge(act_in_ready, j + (gated_base[st] + 1))
                nc.scalar.activation(act_out[:], act_in[:], ACT.Sigmoid).then_inc(act_out_ready, 1)
                if norm + 1 == norms["final"]:
                    gain_hi(act, norm + 1, j)
            each_job(act, st, job)
            if norm + 1 < norms["final"]:
                with act.Fori(0, DT) as d:
                    gain_hi(act, norm + 1, d)

        def ple_vector(dve, st):
            norm, m = norms[st], ple_index[st]
            for k in range(PT):
                dve.wait_ge(emb_hi_ready, PT * m + k + 1)
                nc.vector.tensor_tensor(emb_lo[:, k], bank[5 + k][:], emb_hi[:, k].bitcast(F32),
                                        ALU.subtract).then_inc(emb_ready, 1)
            inverse(dve, norm)
            dve.wait_ge(rinv_ready, norm + 1)

            def job(n, j, slot, ahead):
                dve.wait_ge(job_done, n + 1)
                nc.vector.tensor_tensor(act_in[:], bank[2 * slot][:], rinv[:],
                                        ALU.mult).then_inc(act_in_ready, 1)
                split_lo(dve, n + 2, slot, ahead)
                dve.wait_ge(act_out_ready, j + (gated_base[st] + 1))
                nc.vector.tensor_tensor(prod[:], act_out[:], bank[2 * slot + 1][:],
                                        ALU.mult).then_inc(banks_free, 1)
                dve.wait_ge(banks_free, n + 1)
                nc.vector.tensor_tensor(x[:, ds(j)], x[:, ds(j)], prod[:], ALU.add).then_inc(x_ready, 1)
            each_job(dve, st, job)
            if norm + 1 < norms["final"]:
                with dve.Fori(0, DT) as d:
                    gain_lo(dve, norm + 1, d)

        def out_load(e, st, w_out):
            rows = w_out.rearrange("(k p) c -> p k c", p=P)

            def job(n, j, slot, _):
                e.wait_ge(w_ready, n - 1)
                for k in (0, DT // 2):
                    load_tiles(e, n, slot, k, DT // 2, rows[:, k:k + DT // 2, ds(j * P, P)])
            each_job(e, st + "out", job)

        def out_tensor(pe, st):
            y0 = DT * mixers[st]

            def job(n, j, slot, _):
                first = isinstance(j, int) and j == 0
                pe.wait_ge(w_ready, n + 1)
                pe.wait_ge(banks_free, n - 1)
                product(bank[2 * slot][:], slot, 0, DT, y_hi, y_lo,
                        (lambda k: pe.wait_ge(y_ready, y0 + k + 1)) if first else None
                        ).then_inc(job_done, 1)
            each_job(pe, st + "out", job, peel_first=True)

        def out_scalar(act, st):
            def job(n, j, slot, ahead):
                gain_hi(act, norms[st] + 1, j)
                act.wait_ge(job_done, n + 1)
                split_hi(act, n + 2, slot, ahead)
            each_job(act, st + "out", job)

        def out_vector(dve, st):
            norm = norms[st] + 1

            def job(n, j, slot, ahead):
                dve.wait_ge(job_done, n + 1)
                nc.vector.tensor_tensor(x[:, ds(j)], bank[2 * slot][:], x[:, ds(j)],
                                        ALU.add).then_inc(x_ready, 1)
                dve.wait_ge(x_ready, j + (DT * norm + 1))
                dve.sem_inc(banks_free, 1)
                gain_lo(dve, norm, j)
                split_lo(dve, n + 2, slot, ahead)
            each_job(dve, st + "out", job)

        SWA_Q = SWA_HEADS * HD
        HB = SWA_Q + 2 * P
        RD = RP * P

        FIRST_WINDOW, APART = 18, 24

        def even_load(e, st, w_in):
            base = jobs.phases[st + "in"][0]
            cols = w_in.rearrange("(k p) c -> p k c", p=P)
            pairs = [(SWA_Q, SWA_Q + P), (HB + 3 * RD, HB + 3 * RD + P)]
            for j, pair in enumerate(pairs):
                e.wait_ge(w_ready, base + j - 1)
                for part, col in enumerate(pair):
                    load_tiles(e, base + j, (base + j) % 2, part * DT, DT, cols[:, :, col:col + P])
            for m in range(2):
                n = base + 2 + m
                e.wait_ge(w_ready, n - 1)
                for part in range(2):
                    load_tiles(e, n, n % 2, part * DT, DT, cols[:, :, (2 * m + part) * P:][:, :, 0:P])
            with e.Fori(0, 3 * RP // 4) as i:
                for j in range(2):
                    n = i * 2 + (base + 4 + j)
                    e.wait_ge(w_ready, n - 1)
                    for part in range(2):
                        load_tiles(e, n, (base + j) % 2, part * DT, DT,
                                   cols[:, :, ds(i * (4 * P) + (HB + (2 * j + part) * P), P)])

        def even_tensor(pe, st):
            norm = norms[st]
            base = jobs.phases[st + "in"][0]

            def groups(first, last):
                for g in range(first, last):
                    n = base + g // (2 * DT)
                    slot, k, t = n % 2, g % DT, g % (2 * DT)
                    if t == 0:
                        pe.wait_ge(w_ready, n + 1)
                        pe.wait_ge(banks_free, n - 1)
                    if g < DT:
                        pe.wait_ge(xn_ready, DT * norm + k + 1)
                    dst = bank[2 * slot + t // DT][:]
                    hi, lo = w_hi[slot][:, t], w_lo[slot][:, t]
                    nc.tensor.matmul(dst, hi, xn_hi[:, k], start=k == 0, stop=False)
                    nc.tensor.matmul(dst, lo, xn_hi[:, k], start=False, stop=False)
                    mm = nc.tensor.matmul(dst, hi, xn_lo[:, k], start=False, stop=k == DT - 1)
                    if t == 2 * DT - 1:
                        mm.then_inc(job_done, 1)

            def logits(a, u):
                if u == 0:
                    pe.wait_ge(banks_free, base + 2 + a // 2 + 1)
                    if a:
                        pe.wait_ge(E["swa_logit_ready"], 4 * a)
                else:
                    pe.wait_ge(E["swa_logit_ready"], 4 * a + 2)
                for h in range(2):
                    rows = slice(h * HD, (h + 1) * HD)
                    for n in (2 * u, 2 * u + 1):
                        keys = slice(max(n - 1, 0) * P, (n + 1) * P)
                        width = keys.stop - keys.start
                        c = (n - 2 * u + 1) * 2 * P
                        mm = nc.tensor.matmul(bank[4 + h][:, c - width:c], swa_q[rows, a, n * P:(n + 1) * P],
                                              swa_k[a // 2][rows, keys], start=True, stop=True)
                mm.then_inc(E["swa_qk_done"], 1)

            def transposes(a, u):
                if u:
                    pe.wait_ge(E["swa_pt_copied"], 4 * a + 2)
                elif a:
                    pe.wait_ge(E["swa_pt_copied"], 4 * a)
                    pe.wait_ge(y_ready, y0 + a)
                else:
                    pe.wait_ge(E["swa_vt_copied"], 1)
                for h in range(2):
                    pe.wait_ge(E["swa_p_ready"], 2 * a + h + 1)
                    for kb in (2 * u, 2 * u + 1):
                        for d in range(2 if kb + 1 < NB else 1):
                            c = ((kb - 2 * u) * 2 + d) * P
                            mm = nc.tensor.transpose(bank[6 + h][:, c:c + P],
                                                     swa_p[:, h, kb + d, (1 - d) * P:(2 - d) * P],
                                                     ident[:])
                    mm.then_inc(E["swa_pt_ready"], 1)

            def times_values(a):
                pe.wait_ge(E["swa_pt_copied"], 4 * a + 4)
                cols = slice(a // 2 * HD, (a // 2 + 1) * HD)
                for n in range(NB):
                    for h in range(2):
                        dst = bank[6][h * HD:(h + 1) * HD, n * P:(n + 1) * P]
                        mm = nc.tensor.matmul(dst, swa_vt[:, n, cols], swa_pt[:, h, n, 0],
                                              start=True, stop=n == 0)
                        if n:
                            mm = nc.tensor.matmul(dst, swa_vt[:, n - 1, cols], swa_pt[:, h, n - 1, 1],
                                                  start=False, stop=True)
                mm.then_inc(E["swa_o_done"], 1)

            y0 = DT * mixers[st]
            groups(0, DT)
            mean_square(pe, norm)
            groups(DT, 4 * DT)
            pe.wait_ge(E["swa_v_ready"], 1)
            for b in range(NB):
                mm = nc.tensor.transpose(bank[7][:, b * P:(b + 1) * P], swa_v[:, b * P:(b + 1) * P],
                                         ident[:])
            mm.then_inc(E["swa_vt_ready"], 1)
            for g in range(4 * DT, 4 * DT + FIRST_WINDOW + APART * (RP - 1) + 41):
                for a in range(RP):
                    since = g - (4 * DT + FIRST_WINDOW + APART * a)
                    if since in (0, 5):
                        logits(a, since // 5)
                    elif since in (32, 36):
                        transposes(a, since // 4 - 8)
                    elif since == 40:
                        times_values(a)
                groups(g, min(g + 1, 20 * DT))

        def even_scalar(act, st):
            base = jobs.phases[st + "in"][0]
            y0 = DT * mixers[st]
            root(act, norms[st])

            def step(n):
                act.wait_ge(job_done, n + 1)
                split_hi(act, n + 2, n % 2, jobs.of(n + 2))

            def exponents(a):
                for h in range(2):
                    act.wait_ge(E["swa_nm_ready"], 2 * a + h + 1)
                    if a:
                        act.wait_ge(E["swa_pt_ready"], 4 * a)
                    for n in range(NB):
                        nc.scalar.activation(swa_p[:, h, n], swa_logit[:, h, n], ACT.Exp,
                                             bias=swa_nm[:, h, n:n + 1], accum_out=swa_sum[:, h, n:n + 1])
                    nc.scalar.activation(swa_esink[:, h], swa_nm[:, h], ACT.Exp,
                                         bias=swa_sink[:, 2 * a + h:2 * a + h + 1]
                                         ).then_inc(E["swa_exp_ready"], 1)

            def copy_pt(a, u):
                blocks = 4 - u
                for h in range(2):
                    act.wait_ge(E["swa_pt_ready"], 4 * a + 2 * u + h + 1)
                    nc.scalar.copy(swa_pt[:, h, 2 * u:2 * u + 2].rearrange("p k d q -> p (k d q)")[
                        :, 0:blocks * P], bank[6 + h][:, 0:blocks * P]).then_inc(E["swa_pt_copied"], 1)

            def values_hi(a):
                act.wait_ge(E["swa_o_done"], a + 1)
                nc.scalar.copy(y_hi[:, a], bank[6][:]).then_inc(y_hi_ready, 1)

            step(base)
            step(base + 1)
            act.wait_ge(E["swa_vt_ready"], 1)
            nc.scalar.copy(swa_vt[:], bank[7][:].rearrange("p (b c) -> p b c", b=NB)
                           ).then_inc(E["swa_vt_copied"], 1)
            act.wait_ge(E["lora_ready"], 1)
            nc.scalar.copy(th[HD:P], act_in[HD:P])
            nc.scalar.activation(th[0:HD], act_in[0:HD], ACT.Tanh).then_inc(E["th_ready"], 1)
            act.wait_ge(E["lora_ready"], 2)
            nc.scalar.activation(gate_in[:], other[:], ACT.Sigmoid).then_inc(E["gate_ready"], 1)
            act.wait_ge(E["sink_loaded"], 16)
            def copies(a):
                copy_pt(a, 0)
                copy_pt(a, 1)

            for what in "J0 E0 J1 J2 C0 E1 H0 J3 C1 E2 J4 H1 J5 C2 E3 H2 J6 C3 J7 H3".split():
                k = int(what[1])
                if what[0] == "J":
                    step(base + 2 + k)
                else:
                    {"E": exponents, "C": copies, "H": values_hi}[what[0]](k)

        def even_vector(dve, st):
            norm = norms[st]
            base = jobs.phases[st + "in"][0]
            y0 = DT * mixers[st]
            inverse(dve, norm)
            dve.wait_ge(rinv_ready, norm + 1)
            dve.wait_ge(job_done, base + 1)
            for g in range(2):
                for half in range(2):
                    src = slice(g * HD, (g + 1) * HD)
                    nc.vector.tensor_tensor(swa_k[g][half * HD:(half + 1) * HD],
                                            bank[2 * (base % 2)][src, :], rinv[src], ALU.mult)
            nc.vector.tensor_tensor(swa_v[:], bank[2 * (base % 2) + 1][:], rinv[:],
                                    ALU.mult).then_inc(E["swa_v_ready"], 1)
            dve.wait_ge(E["swa_v_ready"], 1)
            dve.sem_inc(banks_free, 1)
            split_lo(dve, base + 2, base % 2, jobs.of(base + 2))
            dve.wait_ge(job_done, base + 2)
            slot = (base + 1) % 2
            nc.vector.tensor_tensor(lora_in[:, 0, 1:T + 1], bank[2 * slot][:], rinv[:], ALU.mult)
            nc.vector.tensor_tensor(lora_in[:, 1, 1:T + 1], bank[2 * slot + 1][:], rinv[:],
                                    ALU.mult).then_inc(banks_free, 1)
            split_lo(dve, base + 3, slot, jobs.of(base + 3))
            dve.wait_ge(banks_free, base + 2)
            dve.wait_ge(E["lora_zeroed"], 1)
            for t, (diff, mixed) in enumerate(((prod, act_in), (act_out, other))):
                nc.vector.tensor_tensor(diff[:], lora_in[:, t, 0:T], lora_in[:, t, 1:T + 1],
                                        ALU.subtract).then_inc(E["lora_step"], 1)
                dve.wait_ge(E["lora_step"], t + 1)
                mu = rwkv["mu"] + 3 * RP + t
                nc.vector.scalar_tensor_tensor(mixed[:], diff[:], vecs[:, mu:mu + 1],
                                               lora_in[:, t, 1:T + 1], ALU.mult,
                                               ALU.add).then_inc(E["lora_ready"], 1)
            dve.wait_ge(E["sink_loaded"], 16)
            nc.vector.tensor_scalar(nsink[:], swa_sink[:], -1.0, None, ALU.mult
                                    ).then_inc(E["nsink_ready"], 1)

            def logits(a, u):
                if a == 0 and u == 0:
                    dve.wait_ge(E["dist_masked"], 1)
                    dve.wait_ge(E["blank_ready"], 1)
                    dve.wait_ge(E["slope_ready"], SWA_HEADS)
                    dve.wait_ge(E["nsink_ready"], 1)
                if a and u == 0:
                    dve.wait_ge(E["swa_exp_ready"], 2 * a)
                dve.wait_ge(E["swa_qk_done"], 2 * a + u + 1)
                for h in range(2):
                    slope = swa_slope[:, 2 * a + h:2 * a + h + 1]
                    if u == 0:
                        nc.vector.scalar_tensor_tensor(swa_logit[:, h, 0, P:2 * P], swa_dist[:, P:2 * P],
                                                       slope, bank[4 + h][:, P:2 * P], ALU.mult, ALU.add)
                        nc.vector.scalar_tensor_tensor(swa_logit[:, h, 1], swa_dist[:], slope,
                                                       bank[4 + h][:, 2 * P:4 * P], ALU.mult, ALU.add
                                                       ).then_inc(E["swa_logit_ready"], 1)
                    else:
                        dist = swa_dist[:].rearrange("p (o c) -> p o c", o=1).broadcast_to([P, 2, 2 * P])
                        nc.vector.scalar_tensor_tensor(
                            swa_logit[:, h, 2:4], dist, slope,
                            bank[4 + h][:].rearrange("p (o c) -> p o c", o=2), ALU.mult, ALU.add
                        ).then_inc(E["swa_logit_ready"], 1)

            def maxima(a):
                for h in range(2):
                    dve.wait_ge(E["swa_logit_ready"], 4 * a + 3 + h)
                    if a:
                        dve.wait_ge(E["swa_exp_ready"], 2 * a)
                    nc.vector.tensor_reduce(swa_nmax[:, h], swa_logit[:, h], AX.X, ALU.max,
                                            negate=True).then_inc(E["swa_max_ready"], 1)
                for h in range(2):
                    dve.wait_ge(E["swa_max_ready"], 2 * a + h + 1)
                    nc.vector.tensor_scalar(swa_nm[:, h], swa_nmax[:, h],
                                            nsink[:, 2 * a + h:2 * a + h + 1], None, ALU.min
                                            ).then_inc(E["swa_nm_ready"], 1)

            def denominators(a):
                dve.wait_ge(E["swa_exp_ready"], 2 * a + 2)
                if a:
                    dve.wait_ge(E["swa_p_ready"], 2 * a)
                nc.vector.tensor_tensor(swa_den[:], swa_sum[:], swa_esink[:], ALU.add
                                        ).then_inc(E["swa_den_ready"], 1)
                dve.wait_ge(E["swa_den_ready"], a + 1)
                nc.vector.reciprocal(swa_rcp[:], swa_den[:]).then_inc(E["swa_rcp_ready"], 1)

            def values_lo(a):
                dve.wait_ge(y_hi_ready, y0 + a + 1)
                nc.vector.tensor_tensor(y_lo[:, a], bank[6][:], y_hi[:, a].bitcast(F32),
                                        ALU.subtract).then_inc(y_ready, 1)

            def step(k):
                n = base + 2 + k
                dve.wait_ge(job_done, n + 1)
                if k == 2:
                    dve.wait_ge(E["hb_zeroed"], 1)
                for t in range(2):
                    src = bank[2 * (n % 2) + t][:]
                    if k < 2:
                        mm = nc.vector.scalar_tensor_tensor(swa_q[:, 2 * k + t], src, HD ** -0.5, rinv[:],
                                                            ALU.mult, ALU.mult)
                    else:
                        mm = nc.vector.tensor_tensor(hb[:, 2 * (k - 2) + t, 1:T + 1], src, rinv[:],
                                                     ALU.mult)
                mm.then_inc(banks_free, 1)
                split_lo(dve, n + 2, n % 2, jobs.of(n + 2))

            def all_logits(a):
                logits(a, 0)
                logits(a, 1)
                maxima(a)

            for what in "J0 L0 J1 D0 L1 J2 D1 V0 J3 L2 J4 D2 V1 L3 J5 D3 V2 J6 J7 V3".split():
                k = int(what[1])
                {"J": step, "L": all_logits, "D": denominators, "V": values_lo}[what[0]](k)

        def even_pool(pool, st):
            base = jobs.phases[st + "in"][0]
            pool.wait_ge(job_done, base)
            nc.gpsimd.memset(hb[:, :, 0:1], 0.0).then_inc(E["hb_zeroed"], 1)
            nc.gpsimd.memset(lora_in[:, :, 0:1], 0.0).then_inc(E["lora_zeroed"], 1)
            pool.dma_start(swa_sink[:], dram["swa_sinks"].broadcast_to([P, SWA_HEADS])
                           ).then_inc(E["sink_loaded"], 16)
            for h in range(SWA_HEADS):
                nc.gpsimd.memset(swa_slope[:, h:h + 1], -(2.0 ** (-8.0 * (h + 1) / SWA_HEADS))
                                 ).then_inc(E["slope_ready"], 1)
            nc.gpsimd.iota(swa_dist[:], [[-1, 2 * P]], base=P, channel_multiplier=1,
                           allow_small_or_imprecise_dtypes=True).then_inc(E["dist_ready"], 1)
            pool.wait_ge(E["dist_ready"], 1)
            nc.gpsimd.affine_select(out=swa_dist[:], in_=swa_dist[:], compare_op=ALU.is_ge, fill=MASKED,
                                    base=P, pattern=[[-1, 2 * P]], channel_multiplier=1
                                    ).then_inc(E["dist_cut"], 1)
            pool.wait_ge(E["dist_cut"], 1)
            nc.gpsimd.affine_select(out=swa_dist[:], in_=swa_dist[:], compare_op=ALU.is_ge, fill=MASKED,
                                    base=-1, pattern=[[1, 2 * P]], channel_multiplier=-1
                                    ).then_inc(E["dist_masked"], 1)
            for h in range(2):
                mm = nc.gpsimd.memset(swa_logit[:, h, 0, 0:P], -MASKED)
            mm.then_inc(E["blank_ready"], 1)
            rwkv_load(pool)
            rwkv_constants(pool)
            for a in range(RP):
                pool.wait_ge(E["swa_rcp_ready"], a + 1)
                for h in range(2):
                    nc.gpsimd.tensor_tensor(
                        swa_p[:, h], swa_p[:, h],
                        swa_rcp[:, h].rearrange("p (b o) -> p b o", o=1).broadcast_to([P, NB, 2 * P]),
                        ALU.mult).then_inc(E["swa_p_ready"], 1)


        def step(name):
            return next(steps_done[e] for e in RWKV_STEPS if name in RWKV_STEPS[e])

        def due(e, name, h, q):
            steps = next(v for v in RWKV_STEPS.values() if name in v)
            e.wait_ge(step(name), h * (2 * len(steps)) + (2 * steps.index(name) + q + 1))

        def stand_alone(pe):
            pe.sem_inc(rwkv_waited, 1)

        MASK_T, MASK_TI, MASK_0T, MASK_L = 0, 1, 2, 3

        def by_chunk(ap):
            return ap.rearrange("p (c t) -> p c t", t=C)

        def over_chunks(ap, n=NC):
            return ap.rearrange("p (o t) -> p o t", o=1).broadcast_to([P, n, C])

        def ends(q):
            return chunk_end[:, q].rearrange("p (c o) -> p c o", o=1).broadcast_to([P, NC, C])

        def rb(q, k):
            return bank[4 * q + k]

        def vec(name, h, q):
            return vecs[:, ds(h * 2 + (rwkv[name] + q))]

        def rwkv_start(e, st, h):
            e.wait_ge(y_ready, h * 2 + (DT * mixers[st] + RP))
            e.wait_ge(job_done, jobs.phases[st + "out"][0])

        def rwkv_tensor(pe, st):
            def each(dst, operands, width=C, chunks=range(NC)):
                stand_alone(pe)
                for c in chunks:
                    at = (c - chunks[0]) * width
                    for hh in range(2):
                        rows = slice(hh * HD, (hh + 1) * HD)
                        for k, (lhsT, rhs) in enumerate(operands):
                            mm = nc.tensor.matmul(dst[rows, at:at + width], lhsT(c, rows), rhs(c, rows),
                                                  start=k == 0, stop=k == len(operands) - 1)
                return mm

            def transposed(dst, src):
                stand_alone(pe)
                for c in range(NC):
                    cols = slice(c * C, (c + 1) * C)
                    for r in (slice(0, HD), slice(HD, P)):
                        if r.start == 0:
                            nc.tensor.transpose(dst[r, cols], src(c, r), ident[r, r])
                        else:
                            mm = nc.tensor.matmul(dst[r, cols], src(c, r), ident[r, r], start=True, stop=True)
                return mm

            pe.wait_ge(E["th_ready"], 1)
            pe.wait_ge(E["gate_ready"], 1)
            with pe.Fori(0, 2) as h:
                rwkv_start(pe, st, h)
                for q in range(2):
                    due(pe, "weights_staged", h, q)
                    nc.tensor.matmul(rb(q, 0)[:], lora_wa_pair[0:HD, q], th[0:HD], start=True, stop=True)
                    nc.tensor.matmul(rb(q, 1)[:], lora_wa_pair[HD:P, q], th[HD:P], start=True,
                                     stop=True).then_inc(step("lora"), 1)
                for q in range(2):
                    due(pe, "kk_squared", h, q)
                    nc.tensor.matmul(rb(q, 2)[:], head_ones[:], tmp[q][6][:], start=True, stop=True
                                     ).then_inc(step("kk_summed"), 1)
                for q in range(2):
                    due(pe, "v_mixed", h, q)
                    due(pe, "sigmoids", h, q)
                    transposed(rb(q, 0), lambda c, r: tmp[q][7][r, c * C:(c + 1) * C]
                             ).then_inc(step("v_turned"), 1)
                for q in range(2):
                    due(pe, "rk", h, q)
                    nc.tensor.matmul(rb(q, 3)[:], head_ones[:], bonus[:, q], start=True, stop=True
                                     ).then_inc(step("rk_summed"), 1)
                for q in range(2):
                    due(pe, "kq", h, q)
                    transposed(rb(q, 1), lambda c, r: kr[r, q, c, 0]).then_inc(step("kq_turned"), 1)
                for q in range(2):
                    due(pe, "b_tail", h, q)
                    transposed(rb(q, 2), lambda c, r: tmp[q][0][r, c * C:(c + 1) * C]
                             ).then_inc(step("b_turned"), 1)
                for q in range(2):
                    due(pe, "rq", h, q)
                    due(pe, "v_by_token", h, q)
                    due(pe, "kq_by_token", h, q)
                    for half in range(2):
                        mm = each(rb(q, half), [(lambda c, r: bk[r, q, c, 0], lambda c, r: kr[r, q, c])],
                                  2 * C, range(half * NC // 2, (half + 1) * NC // 2))
                    mm.then_inc(step("ab"), 1)
                for q in range(2):
                    due(pe, "k_tail", h, q)
                    due(pe, "bonus", h, q)
                    transposed(rb(q, 3), lambda c, r: tmp[q][2][r, c * C:(c + 1) * C]
                             ).then_inc(step("k_turned"), 1)
                for q in range(2):
                    due(pe, "b_by_token", h, q)
                    due(pe, "k_by_token", h, q)
                    for half in range(2):
                        mm = each(rb(q, 2 + half), [(lambda c, r: bk[r, q, c, 1], lambda c, r: kr[r, q, c])],
                                  2 * C, range(half * NC // 2, (half + 1) * NC // 2))
                    mm.then_inc(step("ak"), 1)
                for q in range(2):
                    due(pe, "ab_masked", h, q)
                    transposed(rb(q, 0), lambda c, r: aw[r, q, c, 1]).then_inc(step("aab"), 1)
                for q in range(2):
                    due(pe, "ak_masked", h, q)
                    each(rb(q, 1), [(lambda c, r: m_inv[r, q, c], lambda c, r: vtok[r, q, c])]
                         ).then_inc(step("f"), 1)
                for level in range(1, LEVELS):
                    for q in range(2):
                        due(pe, f"m_copied{level - 1}" if level > 1 else "m0", h, q)
                        each(rb(q, 2), [(lambda c, r: aw[r, q, c, 1], lambda c, r: m_inv[r, q, c])]
                             ).then_inc(step(f"x{level}"), 1)
                    for q in range(2):
                        due(pe, f"x_masked{level}", h, q)
                        each(rb(q, 0), [(lambda c, r: x1[r, q, c], lambda c, r: mt_inv[r, q, c])]
                             ).then_inc(step(f"mx{level}"), 1)
                    if level + 1 < LEVELS:
                        for q in range(2):
                            due(pe, f"m{level}", h, q)
                            transposed(rb(q, 3), lambda c, r: mt_inv[r, q, c]
                                       ).then_inc(step(f"m_turned{level}"), 1)
                for q in range(2):
                    due(pe, f"m{LEVELS - 1}", h, q)
                    due(pe, "f_copied", h, q)
                    for half in range(2):
                        mm = each(rb(q, 1 + half), [(lambda c, r: mt_inv[r, q, c], lambda c, r: kf[r, q, c])],
                                  2 * C, range(half * NC // 2, (half + 1) * NC // 2))
                    mm.then_inc(step("we"), 1)
                for q in range(2):
                    due(pe, "we_copied", h, q)
                    for half in range(2):
                        mm = each(rb(q, (3, 0)[half]), [(lambda c, r: aw[r, q, c, 0], lambda c, r: ba[r, q, c])],
                                  2 * C, range(half * NC // 2, (half + 1) * NC // 2))
                    mm.then_inc(step("gq"), 1)
                for q in range(2):
                    each(rb(q, 1), [(lambda c, r: ktok[r, q, c], lambda c, r: vtok[r, q, c]),
                                    (lambda c, r: ba[r, q, c, 0], lambda c, r: aw[r, q, c, 1])]
                         ).then_inc(step("h"), 1)
                for q in range(2):
                    each(rb(q, 2), [(lambda c, r: vtok[r, q, c], lambda c, r: ark[r, q, c]),
                                    (lambda c, r: aw[r, q, c, 1], lambda c, r: ba[r, q, c, 1])]
                         ).then_inc(step("yc"), 1)
                for c in range(1, NC - 1):
                    for q in range(2):
                        if c == 1:
                            due(pe, "gq_copied", h, q)
                        due(pe, f"state{c}", h, q)
                        stand_alone(pe)
                        for hh in range(2):
                            r = slice(hh * HD, (hh + 1) * HD)
                            mm = nc.tensor.matmul(rb(q, 3)[r, c * C:(c + 1) * C], bk[r, q, c, 0],
                                                  x1[r, q, c], start=True, stop=True)
                        mm.then_inc(step(f"z{c + 1}"), 1)
                for q in range(2):
                    due(pe, f"state{NC - 1}", h, q)
                    each(rb(q, 0), [(lambda c, r: x1[r, q, c], lambda c, r: bk[r, q, c, 1])]
                         ).then_inc(step("yz"), 1)
                for q in range(2):
                    due(pe, "y_raw", h, q)
                    due(pe, "h_copied", h, q)
                    nc.tensor.matmul(rb(q, 1)[:], head_ones[:], tmp[q][4][:], start=True, stop=True
                                     ).then_inc(step("gn_summed"), 1)
                for q in range(2):
                    nc.tensor.matmul(rb(q, 3)[:], lora_g_pair[:, q], gate_in[:], start=True, stop=True
                                     ).then_inc(step("g"), 1)
                for q in range(2):
                    due(pe, "gn_squared", h, q)
                    due(pe, "yc_copied", h, q)
                    nc.tensor.matmul(rb(q, 2)[:], head_ones[:], tmp[q][6][:], start=True, stop=True
                                     ).then_inc(step("gn_var"), 1)

        def rwkv_scalar(act, st):
            with act.Fori(0, 2) as h:
                def copy(dst, src, name, scale=1.0):
                    nc.scalar.activation(dst, src, ACT.Copy, scale=scale).then_inc(step(name), 1)

                rwkv_start(act, st, h)
                for q in range(2):
                    due(act, "k_mixed", h, q)
                    copy(tmp[q][5][:], tmp[q][4][:], "kk", scale=vec("k_k", h, q))
                for q in range(2):
                    nc.scalar.activation(tmp[q][6][:], tmp[q][4][:], ACT.Square, scale=vec("k_k", h, q)
                                         ).then_inc(step("kk_squared"), 1)
                for q in range(2):
                    due(act, "lora", h, q)
                    nc.scalar.activation(tmp[q][0][:], rb(q, 0)[:], ACT.Sigmoid, bias=vec("w0", h, q))
                    nc.scalar.activation(tmp[q][1][:], rb(q, 1)[:], ACT.Sigmoid,
                                         bias=vec("a0", h, q)).then_inc(step("sigmoids"), 1)
                for q in range(2):
                    due(act, "kk_clamped", h, q)
                    nc.scalar.activation(tmp[q][6][:], tmp[q][6][:], ACT.Sqrt).then_inc(step("kk_norm"), 1)
                for q in range(2):
                    due(act, "lcm", h, q)
                    nc.scalar.activation(tmp[q][3][:], tmp[q][2][:], ACT.Exp, scale=-KAPPA
                                         ).then_inc(step("decay"), 1)
                for q in range(2):
                    nc.scalar.activation(tmp[q][0][:], tmp[q][0][:], ACT.Exp, scale=-KAPPA)
                    nc.scalar.activation(tmp[q][2][:], tmp[q][2][:], ACT.Exp, scale=KAPPA
                                         ).then_inc(step("exps"), 1)
                for q in range(2):
                    due(act, "decay", h, q)
                    copy(chunk_end[:, q], by_chunk(tmp[q][3][:])[:, :, C - 1], "chunk_ends")
                for q in range(2):
                    due(act, "v_turned", h, q)
                    copy(vtok[:, q], by_chunk(rb(q, 0)[:]), "v_by_token")
                for q in range(2):
                    due(act, "kq_turned", h, q)
                    copy(kf[:, q, :, 0], by_chunk(rb(q, 1)[:]), "kq_by_token")
                for q in range(2):
                    due(act, "b_turned", h, q)
                    copy(ba[:, q, :, 0], by_chunk(rb(q, 2)[:]), "b_by_token")
                for q in range(2):
                    due(act, "k_turned", h, q)
                    copy(ktok[:, q], by_chunk(rb(q, 3)[:]), "k_by_token")
                for q in range(2):
                    due(act, "aab", h, q)
                    copy(aw[:, q, :, 0], by_chunk(rb(q, 0)[:]), "aab_copied")
                for q in range(2):
                    due(act, "f", h, q)
                    copy(kf[:, q, :, 1], by_chunk(rb(q, 1)[:]), "f_copied")
                for level in range(1, LEVELS - 1):
                    for q in range(2):
                        due(act, f"m_turned{level}", h, q)
                        copy(m_inv[:, q], by_chunk(rb(q, 3)[:]), f"m_copied{level}")
                for q in range(2):
                    due(act, "we", h, q)
                    for which, scale in ((0, 1.0), (1, -1.0)):
                        for half in range(2):
                            src = rb(q, 1 + half)[:].rearrange("p (c w t) -> p c w t", w=2, t=C)
                            mm = nc.scalar.activation(aw[:, q, half * NC // 2:(half + 1) * NC // 2, which],
                                                      src[:, :, which], ACT.Copy, scale=scale)
                    mm.then_inc(step("we_copied"), 1)
                for q in range(2):
                    due(act, "h", h, q)
                    copy(mt_inv[:, q], by_chunk(rb(q, 1)[:]), "h_copied")
                for q in range(2):
                    due(act, "yc", h, q)
                    copy(ark[:, q], by_chunk(rb(q, 2)[:]), "yc_copied")
                for q in range(2):
                    due(act, "gn_centred", h, q)
                    nc.scalar.activation(tmp[q][6][:], tmp[q][4][:], ACT.Square
                                         ).then_inc(step("gn_squared"), 1)
                for q in range(2):
                    due(act, "gn_var", h, q)
                    nc.scalar.activation(tmp[q][6][:], rb(q, 2)[:], ACT.Sqrt, bias=gn_eps[:],
                                         scale=1.0 / HD).then_inc(step("gn_std"), 1)
                for q in range(2):
                    due(act, "y_done", h, q)
                    nc.scalar.copy(y_hi[:, ds(h * 2 + (RP + q))], tmp[q][5][:]).then_inc(y_hi_ready, 1)

        def rwkv_vector(dve, st):
            y0 = DT * mixers[st]
            with dve.Fori(0, 2) as h:
                def tt(dst, a, b, op, name=None):
                    mm = nc.vector.tensor_tensor(dst, a, b, op)
                    if name:
                        mm.then_inc(step(name), 1)

                def stt(dst, a, scalar, b, op0, op1, name=None):
                    mm = nc.vector.scalar_tensor_tensor(dst, a, scalar, b, op0, op1)
                    if name:
                        mm.then_inc(step(name), 1)

                def projected(t, q):
                    return hb[:, ds(h * 2 + (t * RP + q)), 1:T + 1].rearrange("p o t -> p (o t)")

                def mu(t, q):
                    return vecs[:, ds(h * 2 + (rwkv["mu"] + t * RP + q))]

                rwkv_start(dve, st, h)
                for q in range(2):
                    due(dve, "diff_k", h, q)
                    stt(tmp[q][4][:], tmp[q][4][:], mu(1, q), projected(1, q), ALU.mult, ALU.add, "k_mixed")
                for q in range(2):
                    due(dve, "diff_v", h, q)
                    stt(tmp[q][7][:], tmp[q][7][:], mu(2, q), projected(2, q), ALU.mult, ALU.add, "v_mixed")
                for q in range(2):
                    due(dve, "kk_summed", h, q)
                    nc.vector.tensor_scalar(tmp[q][6][:], rb(q, 2)[:], L2_EPS ** 2, None, ALU.max
                                            ).then_inc(step("kk_clamped"), 1)
                for q in range(2):
                    due(dve, "sigmoids", h, q)
                    nc.vector.tensor_tensor_scan(tmp[q][2][:], chunk_start[:], tmp[q][0][:], 0.0,
                                                 ALU.mult, ALU.add).then_inc(step("lc"), 1)
                for q in range(2):
                    due(dve, "lc", h, q)
                    tt(tmp[q][0][:], tmp[q][2][:], tmp[q][0][:], ALU.subtract, "lcm")
                for q in range(2):
                    due(dve, "diff_r", h, q)
                    stt(kr[:, q, :, 1], kr[:, q, :, 1], mu(0, q), by_chunk(projected(0, q)),
                        ALU.mult, ALU.add, "r_mixed")
                for q in range(2):
                    nc.vector.tensor_scalar(bk[:, q, :, 1], by_chunk(tmp[q][1][:]), 1.0, vec("k_a", h, q),
                                            ALU.subtract, ALU.mult).then_inc(step("ka"), 1)
                for q in range(2):
                    due(dve, "ka", h, q)
                    due(dve, "kk_squared", h, q)
                    stt(by_chunk(tmp[q][4][:]), bk[:, q, :, 1], 1.0, by_chunk(tmp[q][4][:]),
                        ALU.add, ALU.mult, "k")
                for q in range(2):
                    due(dve, "k", h, q)
                    due(dve, "r_mixed", h, q)
                    stt(by_chunk(bonus[:, q]), kr[:, q, :, 1], vec("r_k", h, q), by_chunk(tmp[q][4][:]),
                        ALU.mult, ALU.mult, "rk")
                for q in range(2):
                    due(dve, "kk_norm", h, q)
                    nc.vector.reciprocal(tmp[q][6][:], tmp[q][6][:]).then_inc(step("kk_rinv"), 1)
                for q in range(2):
                    due(dve, "kk_rinv", h, q)
                    tt(tmp[q][5][:], tmp[q][5][:], tmp[q][6][:], ALU.mult, "kkn")
                for q in range(2):
                    due(dve, "kkn", h, q)
                    due(dve, "exps", h, q)
                    tt(kr[:, q, :, 0], by_chunk(tmp[q][5][:]), by_chunk(tmp[q][0][:]), ALU.mult, "kq")
                for q in range(2):
                    tt(tmp[q][5][:], tmp[q][5][:], tmp[q][1][:], ALU.mult, "kka")
                for q in range(2):
                    due(dve, "kka", h, q)
                    tt(bk[:, q, :, 0], by_chunk(tmp[q][5][:]), by_chunk(tmp[q][2][:]), ALU.mult, "b_scaled")
                for q in range(2):
                    tt(kr[:, q, :, 1], kr[:, q, :, 1], by_chunk(tmp[q][3][:]), ALU.mult, "rq")
                for q in range(2):
                    tt(bk[:, q, :, 1], by_chunk(tmp[q][4][:]), by_chunk(tmp[q][2][:]), ALU.mult, "k_scaled")
                for q in range(2):
                    due(dve, "rk_summed", h, q)
                    tt(bonus[:, q], rb(q, 3)[:], tmp[q][7][:], ALU.mult, "bonus")

                def halves(q, first, second):
                    for half, k in enumerate((first, second)):
                        yield (slice(half * NC // 2, (half + 1) * NC // 2),
                               rb(q, k)[:].rearrange("p (c w t) -> p c w t", w=2, t=C))

                def mask(k, n=NC // 2):
                    return over_chunks(masks[:, k], n)

                for q in range(2):
                    due(dve, "ab", h, q)
                    for chunks, src in halves(q, 0, 1):
                        tt(aw[:, q, chunks, 1], src[:, :, 0], mask(MASK_T), ALU.mult)
                    for k, (chunks, src) in enumerate(halves(q, 0, 1)):
                        tt(ba[:, q, chunks, 1], src[:, :, 1], mask(MASK_TI), ALU.mult,
                           "ab_masked" if k else None)
                for q in range(2):
                    due(dve, "ak", h, q)
                    for chunks, src in halves(q, 2, 3):
                        tt(m_inv[:, q, chunks], src[:, :, 0], mask(MASK_T), ALU.mult)
                    for k, (chunks, src) in enumerate(halves(q, 2, 3)):
                        tt(ark[:, q, chunks], src[:, :, 1], mask(MASK_TI), ALU.mult,
                           "ak_masked" if k else None)
                for q in range(2):
                    due(dve, "aab_copied", h, q)
                    tt(x1[:, q], aw[:, q, :, 0], mask(MASK_L, NC), ALU.mult, "init")
                for q in range(2):
                    tt(mt_inv[:, q], aw[:, q, :, 1], mask(MASK_0T, NC), ALU.mult, "init_t")
                for q in range(2):
                    due(dve, "init_t", h, q)
                    due(dve, "f", h, q)
                    tt(m_inv[:, q], over_chunks(eye[:]), x1[:, q], ALU.subtract)
                    tt(mt_inv[:, q], over_chunks(eye[:]), mt_inv[:, q], ALU.subtract, "m0")
                for level in range(1, LEVELS):
                    for q in range(2):
                        due(dve, f"x{level}", h, q)
                        tt(x1[:, q], by_chunk(rb(q, 2)[:]), mask(MASK_L + level, NC), ALU.mult, f"x_masked{level}")
                    for q in range(2):
                        due(dve, f"mx{level}", h, q)
                        tt(mt_inv[:, q], mt_inv[:, q], by_chunk(rb(q, 0)[:]), ALU.subtract, f"m{level}")
                for q in range(2):
                    due(dve, "gq", h, q)
                    due(dve, "diag", h, q)
                    for chunks, src in halves(q, 3, 0):
                        tt(bk[:, q, chunks, 0], by_chunk(tmp[q][3][:])[:, chunks], src[:, :, 0],
                           ALU.subtract)
                    for k, (chunks, src) in enumerate(halves(q, 3, 0)):
                        tt(bk[:, q, chunks, 1], kr[:, q, chunks, 1], src[:, :, 1], ALU.subtract,
                           "gq_copied" if k else None)
                for q in range(2):
                    nc.vector.memset(x1[:, q, 0], 0.0)
                    due(dve, "h_copied", h, q)
                    nc.vector.tensor_copy(x1[:, q, 1], mt_inv[:, q, 0]).then_inc(step("state1"), 1)
                for c in range(1, NC - 1):
                    for q in range(2):
                        due(dve, f"z{c + 1}", h, q)
                        tt(x1[:, q, c + 1], rb(q, 3)[:, c * C:(c + 1) * C], mt_inv[:, q, c], ALU.add,
                           f"state{c + 1}")
                for q in range(2):
                    due(dve, "yz", h, q)
                    due(dve, "yc_copied", h, q)
                    tt(by_chunk(tmp[q][4][:]), by_chunk(rb(q, 0)[:]), ark[:, q], ALU.add, "y_raw")
                for q in range(2):
                    due(dve, "y_raw", h, q)
                    due(dve, "gn_summed", h, q)
                    stt(tmp[q][4][:], rb(q, 1)[:], -1.0 / HD, tmp[q][4][:], ALU.mult, ALU.add, "gn_centred")
                for q in range(2):
                    due(dve, "gn_centred", h, q)
                    due(dve, "g", h, q)
                    stt(tmp[q][5][:], tmp[q][4][:], vec("ln_w", h, q), rb(q, 3)[:], ALU.mult, ALU.mult,
                        "y_weighted")
                for q in range(2):
                    stt(bonus[:, q], bonus[:, q], vec("ln_b", h, q), rb(q, 3)[:], ALU.add, ALU.mult,
                        "bonus_gated")
                for q in range(2):
                    due(dve, "gn_std", h, q)
                    nc.vector.reciprocal(tmp[q][6][:], tmp[q][6][:]).then_inc(step("gn_rinv"), 1)
                for q in range(2):
                    due(dve, "gn_rinv", h, q)
                    tt(tmp[q][5][:], tmp[q][5][:], tmp[q][6][:], ALU.mult, "gn_normed")
                for q in range(2):
                    due(dve, "gn_normed", h, q)
                    tt(tmp[q][5][:], tmp[q][5][:], bonus[:, q], ALU.add, "y_done")
                for q in range(2):
                    dve.wait_ge(y_hi_ready, h * 2 + (y0 + RP + q + 1))
                    nc.vector.tensor_tensor(y_lo[:, ds(h * 2 + (RP + q))], tmp[q][5][:],
                                            y_hi[:, ds(h * 2 + (RP + q))].bitcast(F32), ALU.subtract
                                            ).then_inc(y_ready, 1)

        def rwkv_constants(pool):
            filled = [0]

            def fill(*instructions):
                for step in instructions:
                    step().then_inc(E["masks_filled"], 1)
                    filled[0] += 1
                    pool.wait_ge(E["masks_filled"], filled[0])

            def select(m, op, base, pattern, channel):
                for hh in range(2):
                    half = m[hh * HD:(hh + 1) * HD]
                    fill(lambda: nc.gpsimd.affine_select(out=half, in_=half, compare_op=op, fill=0.0,
                                                         base=base, pattern=pattern,
                                                         channel_multiplier=channel))

            fill(lambda: nc.gpsimd.memset(masks[:], 1.0), lambda: nc.gpsimd.memset(eye[:], 1.0),
                 lambda: nc.gpsimd.memset(chunk_start[:], 1.0),
                 lambda: nc.gpsimd.memset(by_chunk(chunk_start[:])[:, :, 0:1], 0.0),
                 lambda: nc.gpsimd.memset(head_ones[:], 0.0),
                 lambda: nc.gpsimd.memset(head_ones[0:HD, 0:HD], 1.0),
                 lambda: nc.gpsimd.memset(head_ones[HD:P, HD:P], 1.0),
                 lambda: nc.gpsimd.memset(gn_eps[:], GN_EPS))
            select(eye, ALU.is_equal, 0, [[-1, C]], 1)
            select(masks[:, MASK_T], ALU.is_gt, 0, [[1, C]], -1)
            select(masks[:, MASK_TI], ALU.is_ge, 0, [[1, C]], -1)
            for level in range(LEVELS):
                k = 1 << level
                blocks = C // (2 * k)
                m = masks[:, MASK_L + level].rearrange("p (b t) -> p b t", t=2 * k)
                select(m, ALU.is_ge, -k, [[-2 * k, blocks], [0, 2 * k]], 1)
                select(m, ALU.is_ge, 2 * k - 1, [[2 * k, blocks], [0, 2 * k]], -1)
                select(m, ALU.is_ge, k - 1, [[0, blocks], [-1, 2 * k]], 0)
            m = masks[:, MASK_0T].rearrange("p (b t) -> p b t", t=2)
            select(m, ALU.is_ge, 0, [[-2, C // 2], [0, 2]], 1)
            select(m, ALU.is_ge, 0, [[2, C // 2], [0, 2]], -1)
            select(m, ALU.is_ge, -1, [[0, C // 2], [1, 2]], 0)

        def rwkv_load(pool):
            for dst, src in ((lora_wa[0:HD], "rwkv_w2"), (lora_wa[HD:P], "rwkv_a2"), (lora_g[:], "rwkv_g2")):
                pool.dma_start(dst, dram[src][0]).then_inc(E["lora_loaded"], 16)

        def rwkv_pool(pool, st):
            pool.wait_ge(E["lora_loaded"], 48)
            with pool.Fori(0, 2) as h:
                rwkv_start(pool, st, h)
                for q in range(2):
                    cols = lambda m: m[:, ds(h * (2 * P) + q * P, P)]
                    nc.gpsimd.tensor_copy(lora_wa_pair[:, q], cols(lora_wa))
                    nc.gpsimd.tensor_copy(lora_g_pair[:, q], cols(lora_g)).then_inc(step("weights_staged"), 1)
                for t in (1, 2, 0):
                    for q in range(2):
                        i = ds(h * 2 + (t * RP + q))
                        before = hb[:, i, 0:T].rearrange("p o t -> p (o t)")
                        here = hb[:, i, 1:T + 1].rearrange("p o t -> p (o t)")
                        if t == 0:
                            dst, before, here = kr[:, q, :, 1], by_chunk(before), by_chunk(here)
                        else:
                            dst = tmp[q][4 if t == 1 else 7][:]
                        nc.gpsimd.tensor_tensor(dst, before, here, ALU.subtract
                                                ).then_inc(step("diff_k"), 1)
                for q in range(2):
                    due(pool, "b_scaled", h, q)
                    due(pool, "chunk_ends", h, q)
                    nc.gpsimd.tensor_tensor(by_chunk(tmp[q][0][:]), bk[:, q, :, 0], ends(q), ALU.mult
                                            ).then_inc(step("b_tail"), 1)
                for q in range(2):
                    due(pool, "k_scaled", h, q)
                    nc.gpsimd.tensor_tensor(by_chunk(tmp[q][2][:]), bk[:, q, :, 1], ends(q), ALU.mult
                                            ).then_inc(step("k_tail"), 1)
                for q in range(2):
                    due(pool, "rq", h, q)
                    nc.gpsimd.tensor_tensor(by_chunk(tmp[q][3][:]), over_chunks(eye[:]), ends(q), ALU.mult
                                            ).then_inc(step("diag"), 1)
        def unit_cols(u):
            qb = NB - 1 - u
            return qb * (qb + 1) // 2 * P, (qb + 1) * P

        def fox_load(e, st, w_in):
            base = jobs.phases[st + "in"][0]
            cols = w_in.rearrange("(k p) c -> p k c", p=P)
            e.wait_ge(w_ready, base - 1)
            slot = base % 2
            e.dma_start(w_raw[slot][:, 0:DT, 0:FOX_HEADS],
                        cols[:, :, 3 * DM:3 * DM + FOX_HEADS]).then_inc(w_loaded[slot], 16)
            e.dma_start(w_raw[slot][:, 0:DT, FOX_HEADS:P],
                        cols[:, :, 0:P - FOX_HEADS]).then_inc(w_loaded[slot], 16)
            with e.Fori(0, PAIRS) as i:
                n = i * 2 + (base + 1)
                slot = (base + 1) % 2
                e.wait_ge(w_ready, n - 1)
                for part in range(2):
                    load_tiles(e, n, slot, part * DT, DT, cols[:, :, ds(i * P + part * DM, P)])
                e.wait_ge(w_ready, n)
                for k in (0, DT // 2):
                    load_tiles(e, n + 1, 1 - slot, k, DT // 2,
                               cols[:, k:k + DT // 2, ds(i * P + 2 * DM, P)])

        def fox_tensor(pe, st):
            norm = norms[st]
            base = jobs.phases[st + "in"][0]
            slot = base % 2
            pe.wait_ge(w_ready, base + 1)
            pe.wait_ge(banks_free, base - 1)
            product(bank[2 * slot][:], slot, 0, DT, xn_hi, xn_lo,
                    lambda k: pe.wait_ge(xn_ready, DT * norm + k + 1)).then_inc(job_done, 1)
            mean_square(pe, norm)

            def iteration(i, project, attend, multiply):
                n = i * 2 + (base + 1)
                a = i - 1
                slot = (base + 1) % 2

                def groups(first, last):
                    if not project:
                        return
                    for g in range(first, last):
                        job, k = g // (2 * DT), g % DT
                        sl = slot if job == 0 else 1 - slot
                        if g == 0 or g == 2 * DT:
                            pe.wait_ge(w_ready, n + job + 1)
                            pe.wait_ge(banks_free, n + job - 1)
                        dst = bank[2 * sl + (g // DT) % 2][:]
                        w = g % (2 * DT)
                        hi, lo = w_hi[sl][:, w], w_lo[sl][:, w]
                        nc.tensor.matmul(dst, hi, xn_hi[:, k], start=k == 0, stop=False)
                        nc.tensor.matmul(dst, lo, xn_hi[:, k], start=False, stop=False)
                        mm = nc.tensor.matmul(dst, hi, xn_lo[:, k], start=False, stop=k == DT - 1)
                        if g == 2 * DT - 1 or g == 3 * DT - 1:
                            mm.then_inc(job_done, 1)

                def logits(u):
                    if not attend:
                        return
                    if u == 0:
                        pe.wait_ge(banks_free, n - 1)
                        pe.wait_ge(logit_ready, a * (2 * NB)) if not isinstance(a, int) or a else None
                    else:
                        pe.wait_ge(logit_ready, a * (2 * NB) + 2 * u)
                    qb = NB - 1 - u
                    for h in range(2):
                        rows = slice(h * HD, (h + 1) * HD)
                        mm = nc.tensor.matmul(bank[4 + h][:, 0:(qb + 1) * P],
                                              fox_q[rows, qb * P:(qb + 1) * P],
                                              fox_k[rows, 0:(qb + 1) * P], start=True, stop=True)
                    mm.then_inc(qk_done, 1)

                def transposes(u):
                    if not attend:
                        return
                    qb = NB - 1 - u
                    at, _ = unit_cols(u)
                    if u == 0:
                        pe.wait_ge(vt_copied, a + 1)
                        if multiply:
                            pe.wait_ge(y_ready, y0 + a)
                    else:
                        pe.wait_ge(pt_copied, a * (2 * NB) + 2 * u)
                    for h in range(2):
                        pe.wait_ge(p_ready, a * (2 * NB) + (2 * u + h + 1))
                        for kb in range(qb + 1):
                            mm = nc.tensor.transpose(bank[6 + h][:, kb * P:(kb + 1) * P],
                                                     fox_logit[:, h, at + kb * P:at + (kb + 1) * P],
                                                     ident[:])
                        mm.then_inc(pt_ready, 1)

                def times_values():
                    if not multiply:
                        return
                    pe.wait_ge(pt_copied, a * (2 * NB))
                    for kb in range(NB):
                        for h in range(2):
                            mm = nc.tensor.matmul(bank[6][h * HD:(h + 1) * HD, kb * P:T],
                                                  fox_vt[:, kb, h * HD:(h + 1) * HD],
                                                  fox_pt[:, h, kb, kb * P:T],
                                                  start=kb == 0, stop=kb == NB - 1)
                    mm.then_inc(o_done, 1)

                def value_rows():
                    if not attend:
                        return
                    pe.wait_ge(v_ready, a + 1)
                    if isinstance(a, int) and a == 0:
                        pass
                    else:
                        pe.wait_ge(pt_copied, a * (2 * NB))
                    for b in range(NB):
                        mm = nc.tensor.transpose(bank[7][:, b * P:(b + 1) * P],
                                                 fox_v[:, b * P:(b + 1) * P], ident[:])
                    mm.then_inc(vt_ready, 1)

                logits(0)
                groups(0, 2)
                times_values()
                groups(2, 3)
                value_rows()
                groups(3, 5)
                logits(1)
                groups(5, 8)
                logits(2)
                groups(8, 10)
                logits(3)
                groups(10, 12)
                transposes(0)
                groups(12, 15)
                transposes(1)
                groups(15, 18)
                transposes(2)
                groups(18, 21)
                transposes(3)
                groups(21, 24)

            y0 = DT * mixers[st]
            iteration(0, True, False, False)
            pe.wait_ge(cum_ready, 1)
            for b in range(NB):
                mm = nc.tensor.transpose(bank[5][:, b * FOX_HEADS:(b + 1) * FOX_HEADS],
                                         fox_cum[:, b * P:(b + 1) * P], ident[0:FOX_HEADS, 0:FOX_HEADS])
            mm.then_inc(cq_t_ready, 1)
            pe.wait_ge(cq_ready, 1)
            iteration(1, True, True, False)
            with pe.Fori(2, PAIRS) as i:
                iteration(i, True, True, True)
            iteration(PAIRS, False, True, True)
            pe.wait_ge(pt_copied, PAIRS * 2 * NB)
            for kb in range(NB):
                for h in range(2):
                    mm = nc.tensor.matmul(bank[6][h * HD:(h + 1) * HD, kb * P:T],
                                          fox_vt[:, kb, h * HD:(h + 1) * HD],
                                          fox_pt[:, h, kb, kb * P:T], start=kb == 0, stop=kb == NB - 1)
            mm.then_inc(o_done, 1)

        def fox_scalar(act, st):
            norm = norms[st]
            base = jobs.phases[st + "in"][0]
            slot = base % 2
            y0 = DT * mixers[st]
            root(act, norm)
            act.wait_ge(z_neg_ready, 1)
            nc.scalar.activation(act_out[0:FOX_HEADS], other[0:FOX_HEADS], ACT.Exp).then_inc(z_exp_ready, 1)
            act.wait_ge(z_exp_ready, 1)
            nc.scalar.activation(prod[0:FOX_HEADS], act_out[0:FOX_HEADS], ACT.Ln,
                                 bias=ones[0:FOX_HEADS, 0:1]).then_inc(z_log_ready, 1)
            act.wait_ge(job_done, base + 1)
            split_hi(act, base + 2, slot, jobs.of(base + 2))

            def values_hi(a):
                act.wait_ge(o_done, a + 1)
                nc.scalar.copy(y_hi[:, ds(a)], bank[6][:]).then_inc(y_hi_ready, 1)

            def iteration(i, project, attend, multiply, ahead_a, ahead_b):
                n = i * 2 + (base + 1)
                a = i - 1
                slot_a = (base + 1) % 2

                def exponent(u):
                    if not attend:
                        return
                    qb = NB - 1 - u
                    at, cols = unit_cols(u)
                    for h in range(2):
                        act.wait_ge(max_ready, a * (2 * NB) + (2 * u + h + 1))
                        nc.scalar.activation(fox_logit[:, h, at:at + cols], fox_logit[:, h, at:at + cols],
                                             ACT.Exp, bias=fox_nmax[:, qb, h:h + 1],
                                             accum_out=fox_sum[:, qb, h:h + 1]).then_inc(exp_ready, 1)

                def copy_pt(u):
                    if not attend:
                        return
                    qb = NB - 1 - u
                    for h in range(2):
                        act.wait_ge(pt_ready, a * (2 * NB) + (2 * u + h + 1))
                        nc.scalar.copy(fox_pt[:, h, 0:qb + 1, qb * P:(qb + 1) * P],
                                       bank[6 + h][:, 0:(qb + 1) * P].rearrange("p (k q) -> p k q", q=P)
                                       ).then_inc(pt_copied, 1)

                if project:
                    if not (isinstance(i, int) and i == 0):
                        act.wait_ge(job_done, n)
                        split_hi(act, n + 1, 1 - slot_a, ahead_b)
                elif not project:
                    act.wait_ge(job_done, n)
                    split_hi(act, n + 1, 1 - slot_a, ahead_b)
                exponent(0)
                if multiply:
                    values_hi(a - 1)
                exponent(1)
                if attend:
                    act.wait_ge(vt_ready, a + 1)
                    nc.scalar.copy(fox_vt[:], bank[7][:].rearrange("p (b c) -> p b c", b=NB)
                                   ).then_inc(vt_copied, 1)
                exponent(2)
                exponent(3)
                copy_pt(0)
                copy_pt(1)
                if project:
                    act.wait_ge(job_done, n + 1)
                    split_hi(act, n + 2, slot_a, ahead_a)
                copy_pt(2)
                copy_pt(3)

            A, B = 2 * DT, DT
            out0, out1 = jobs.of(base + 1 + 2 * PAIRS), jobs.of(base + 2 + 2 * PAIRS)
            iteration(0, True, False, False, A, None)
            iteration(1, True, True, False, A, B)
            with act.Fori(2, PAIRS - 1) as i:
                iteration(i, True, True, True, A, B)
            iteration(PAIRS - 1, True, True, True, out0, B)
            iteration(PAIRS, False, True, True, None, out1)
            values_hi(PAIRS - 1)

        def fox_vector(dve, st):
            norm = norms[st]
            base = jobs.phases[st + "in"][0]
            slot = base % 2
            y0 = DT * mixers[st]
            inverse(dve, norm)
            dve.wait_ge(rinv_ready, norm + 1)
            g = slice(0, FOX_HEADS)
            dve.wait_ge(job_done, base + 1)
            nc.vector.tensor_tensor(act_in[g], bank[2 * slot][g, :], rinv[g], ALU.mult).then_inc(banks_free, 1)
            dve.wait_ge(banks_free, base + 1)
            dve.wait_ge(bf_loaded, 16)
            nc.vector.tensor_scalar(act_in[g], act_in[g], fox_bf[:], None, ALU.add).then_inc(z_ready, 1)
            dve.wait_ge(z_ready, 1)
            nc.vector.scalar_tensor_tensor(other[g], act_in[g], -1.0, act_in[g], ALU.mult,
                                           ALU.min).then_inc(z_neg_ready, 1)
            dve.wait_ge(z_log_ready, 1)
            nc.vector.scalar_tensor_tensor(rms[g], act_in[g], 0.0, prod[g], ALU.min,
                                           ALU.subtract).then_inc(log_f_ready, 1)
            dve.wait_ge(log_f_ready, 1)
            nc.vector.memset(act_out[g], 1.0).then_inc(ones_row_ready, 1)
            dve.wait_ge(ones_row_ready, 1)
            nc.vector.tensor_tensor_scan(fox_cum[:], act_out[g], rms[g], 0.0, ALU.mult,
                                         ALU.add).then_inc(cum_ready, 1)
            split_lo(dve, base + 2, slot, jobs.of(base + 2))

            def values_lo(a):
                dve.wait_ge(y_hi_ready, a + (y0 + 1))
                nc.vector.tensor_tensor(y_lo[:, ds(a)], bank[6][:], y_hi[:, ds(a)].bitcast(F32),
                                        ALU.subtract).then_inc(y_ready, 1)

            def iteration(i, project, attend, multiply, ahead_a, ahead_b):
                n = i * 2 + (base + 1)
                a = i - 1
                slot_a = (base + 1) % 2

                def logits(u):
                    if not attend:
                        return
                    qb = NB - 1 - u
                    at, cols = unit_cols(u)
                    dve.wait_ge(qk_done, a * NB + (u + 1))
                    if u == 0:
                        dve.wait_ge(cm_ready, a + 1)
                    cq = [fox_cq[:, qb, ds(a * 2 + h)] for h in range(2)]
                    for h in range(2):
                        if qb:
                            nc.vector.scalar_tensor_tensor(
                                fox_logit[:, h, at:at + qb * P], bank[4 + h][:, 0:qb * P], cq[h],
                                fox_c[:, h, 0:qb * P], ALU.add, ALU.subtract)
                        nc.vector.scalar_tensor_tensor(
                            fox_logit[:, h, at + qb * P:at + cols], bank[4 + h][:, qb * P:cols], cq[h],
                            fox_cm[:, h, qb], ALU.add, ALU.subtract).then_inc(logit_ready, 1)
                    for h in range(2):
                        dve.wait_ge(logit_ready, a * (2 * NB) + (2 * u + h + 1))
                        nc.vector.tensor_reduce(fox_nmax[:, qb, h:h + 1], fox_logit[:, h, at:at + cols],
                                                AX.X, ALU.max, negate=True).then_inc(max_ready, 1)

                def inverse_sum(u):
                    if not attend:
                        return
                    qb = NB - 1 - u
                    dve.wait_ge(exp_ready, a * (2 * NB) + 2 * (u + 1))
                    nc.vector.reciprocal(fox_rcp[:, qb], fox_sum[:, qb]).then_inc(rcp_ready, 1)

                if not (isinstance(i, int) and i == 0):
                    dve.wait_ge(job_done, n)
                    nc.vector.tensor_tensor(fox_v[:], bank[2 * (1 - slot_a)][:], rinv[:],
                                            ALU.mult).then_inc(v_ready, 1)
                    dve.wait_ge(v_ready, i)
                    dve.sem_inc(banks_free, 1)
                    split_lo(dve, n + 1, 1 - slot_a, ahead_b)
                logits(0)
                logits(1)
                inverse_sum(0)
                if multiply:
                    values_lo(a - 1)
                logits(2)
                inverse_sum(1)
                logits(3)
                inverse_sum(2)
                inverse_sum(3)
                if project:
                    dve.wait_ge(job_done, n + 1)
                    nc.vector.scalar_tensor_tensor(fox_q[:], bank[2 * slot_a][:], HD ** -0.5, rinv[:],
                                                   ALU.mult, ALU.mult)
                    nc.vector.tensor_tensor(fox_k[:], bank[2 * slot_a + 1][:], rinv[:],
                                            ALU.mult).then_inc(banks_free, 1)
                    split_lo(dve, n + 2, slot_a, ahead_a)

            A, B = 2 * DT, DT
            out0, out1 = jobs.of(base + 1 + 2 * PAIRS), jobs.of(base + 2 + 2 * PAIRS)
            iteration(0, True, False, False, A, None)
            dve.wait_ge(cq_t_ready, 1)
            nc.vector.tensor_copy(fox_cq[:], bank[5][:, 0:NB * FOX_HEADS].rearrange(
                "p (b h) -> p b h", b=NB)).then_inc(cq_ready, 1)
            dve.wait_ge(cq_ready, 1)
            iteration(1, True, True, False, A, B)
            with dve.Fori(2, PAIRS - 1) as i:
                iteration(i, True, True, True, A, B)
            iteration(PAIRS - 1, True, True, True, out0, B)
            iteration(PAIRS, False, True, True, None, out1)
            values_lo(PAIRS - 1)

        def fox_pool(pool, st):
            base = jobs.phases[st + "in"][0]
            pool.wait_ge(job_done, base)
            nc.gpsimd.memset(causal[:], 0.0).then_inc(causal_ready, 1)
            pool.wait_ge(causal_ready, 1)
            nc.gpsimd.affine_select(out=causal[:], in_=causal[:], compare_op=ALU.is_ge, fill=MASKED,
                                    base=0, pattern=[[-1, P]], channel_multiplier=1
                                    ).then_inc(causal_ready, 1)
            pool.wait_ge(causal_ready, 2)
            pool.dma_start(fox_bf[:], dram["fox_b_f"][0].rearrange("(h a) -> h a", a=1)).then_inc(bf_loaded, 16)
            pool.wait_ge(cum_ready, 1)
            pool.dma_start(cum_dram, fox_cum[:]).then_inc(cum_stored, 16)
            pool.wait_ge(cum_stored, 16)

            def pair(a, not_first):
                if not_first:
                    pool.wait_ge(logit_ready, a * (2 * NB))
                src = cum_dram[ds(a * 2, 2)].rearrange("(o h) t -> o h t", o=1).broadcast_to([P, 2, T])
                pool.dma_start(fox_c[:], src).then_inc(c_loaded, 16)
                pool.wait_ge(c_loaded, a * 16 + 16)
                mask = causal[:].rearrange("p (o c) -> p o c", o=1).broadcast_to([P, 2 * NB, P])
                nc.gpsimd.tensor_tensor(fox_cm[:].rearrange("p h b c -> p (h b) c"),
                                        fox_c[:].rearrange("p h (b c) -> p (h b) c", c=P), mask,
                                        ALU.add).then_inc(cm_ready, 1)
                for u in range(NB):
                    at, cols = unit_cols(u)
                    pool.wait_ge(rcp_ready, a * NB + (u + 1))
                    for h in range(2):
                        nc.gpsimd.tensor_tensor(
                            fox_logit[:, h, at:at + cols], fox_logit[:, h, at:at + cols],
                            fox_rcp[:, NB - 1 - u, h:h + 1].broadcast_to([P, cols]), ALU.mult
                        ).then_inc(p_ready, 1)

            pair(0, False)
            with pool.Fori(1, PAIRS) as a:
                pair(a, True)

        final = norms["final"]
        def out_bank(q):
            return bank[(5, 6, 7, 0, 1, 2, 3, 5)[q]]

        def out_rows(q):
            return rows_out[:, q % NB, q // NB * T:(q // NB + 1) * T]

        first_jobs = range(jobs.FIRST, jobs.FIRST + 2)

        @block.sync
        def _(sp):
            for b in range(T // P):
                sp.dma_start(rows_in[:, b], dram["x"][0, b * P:(b + 1) * P, :]).then_inc(rows_loaded[b], 16)
            for st in stages:
                layer = int(st[-1])
                if st.startswith("ffn"):
                    ffn_load(sp, st, dram[st[:4] + "_w_gu"][layer], dram[st[:4] + "_w_down"][layer])
                elif st.startswith("ple"):
                    ple_load(sp, st, dram["ple_w_gate"][layer], dram["ple_w_proj"][layer])
                elif st.startswith("even"):
                    even_load(sp, st, dram["even_w_in"][0])
                    out_load(sp, st, dram["even_w_out"][0])
                elif st.startswith("fox"):
                    fox_load(sp, st, dram["fox_w_in"][0])
                    out_load(sp, st, dram["fox_w_out"][0])
            for q in range(2 * NB):
                half, b = divmod(q, NB)
                sp.wait_ge(ot_by_scalar if q % 2 else ot_by_vector, q // 2 + 1)
                sp.dma_start(out[0, b * P:(b + 1) * P, half * T:(half + 1) * T], out_rows(q)
                             ).then_inc(out_stored, 16)
            sp.wait_ge(out_stored, 16 * 2 * NB)

        @block.gpsimd
        def _(pool):
            nc.gpsimd.memset(ones[:], 1.0).then_inc(consts_ready, 1)
            nc.gpsimd.memset(eps_col[:], EPS).then_inc(consts_ready, 1)
            pool.wait_ge(consts_ready, 1)
            nc.gpsimd.affine_select(out=ident[:], in_=ones[:], compare_op=ALU.is_equal, fill=0.0, base=0,
                                    pattern=[[-1, P]], channel_multiplier=1).then_inc(consts_ready, 1)
            for st in stages:
                if st.startswith("ple"):
                    ple_load_rows(pool, st, dram["p"][int(st[-1]), 0])
                square_sum(pool, norms[st])
                if st.startswith("even"):
                    even_pool(pool, st)
                    rwkv_pool(pool, st)
                elif st.startswith("fox"):
                    fox_pool(pool, st)
            square_sum(pool, final)

        @block.tensor
        def _(pe):
            pe.sem_inc(job_done, jobs.FIRST)
            pe.wait_ge(consts_ready, 3)
            for d in range(DT):
                if d == 4:
                    pe.wait_ge(vecs_loaded, 16 * len(vectors))
                    nc.tensor.transpose(bank[0][:, 0:VECS], vec_rows[:], ident[0:VECS, 0:VECS]
                                        ).then_inc(vecs_t_ready, 1)
                if d >= 4:
                    pe.wait_ge(x_ready, d - 3)
                for b in range(T // P):
                    if d == 0:
                        pe.wait_ge(rows_loaded[b], 16)
                    last = nc.tensor.transpose(bank[4 + d % 4][:, b * P:(b + 1) * P],
                                               rows_in[:, b, d * P:(d + 1) * P], ident[:])
                last.then_inc(xt_ready, 1)
            for st in stages:
                if st.startswith("ffn"):
                    ffn_tensor(pe, st)
                elif st.startswith("ple"):
                    ple_tensor(pe, st)
                elif st.startswith("even"):
                    even_tensor(pe, st)
                    rwkv_tensor(pe, st)
                    out_tensor(pe, st)
                elif st.startswith("fox"):
                    fox_tensor(pe, st)
                    out_tensor(pe, st)
            for q in range(2 * NB):
                half, b = divmod(q, NB)
                if q == 3:
                    pe.wait_ge(sq_sum_ready, DT * (final + 1))
                    pe.wait_ge(rms_ready, final)
                    for k in range(NB):
                        mm = nc.tensor.matmul(bank[4][:, k:k + 1], sq_sum[:, k * P:(k + 1) * P],
                                              ones[:, 0:1], start=True, stop=True)
                    mm.then_inc(ms_ready, 1)
                    pe.wait_ge(banks_free, jobs.FIRST + len(jobs.tiles))
                if q == 7:
                    pe.wait_ge(ot_by_vector, 1)
                for k in range(4):
                    d = 4 * half + k
                    if b == 0:
                        pe.wait_ge(scaled_ready, d + 1)
                    last = nc.tensor.transpose(out_bank(q)[:, k * P:(k + 1) * P],
                                               scaled[:, d, b * P:(b + 1) * P], ident[:])
                last.then_inc(ot_ready, 1)

        @block.scalar
        def _(act):
            row = 0
            for v in vectors:
                act.dma_start(vec_rows[row:row + v.shape[0] // P, :],
                              v.rearrange("(d p) -> d p", p=P)).then_inc(vecs_loaded, 16)
                row += v.shape[0] // P
            act.sem_inc(w_hi_ready, jobs.FIRST)
            act.wait_ge(vecs_ready, 1)
            for d in range(DT):
                if d in (1, 4):
                    n = first_jobs[d // 4]
                    split_hi(act, n, n % 2, jobs.of(n))
                gain_hi(act, 0, d)
            for st in stages:
                if st.startswith("ffn"):
                    ffn_scalar(act, st)
                elif st.startswith("ple"):
                    ple_scalar(act, st)
                elif st.startswith("even"):
                    even_scalar(act, st)
                    rwkv_scalar(act, st)
                    out_scalar(act, st)
                elif st.startswith("fox"):
                    fox_scalar(act, st)
                    out_scalar(act, st)
            act.wait_ge(ms_ready, final + 1)
            act.wait_ge(rinv_ready, final)
            nc.scalar.activation(rms[:, 0:NB], bank[4][:, 0:NB], ACT.Sqrt, bias=eps_col[:],
                                 scale=1.0 / DM).then_inc(rms_ready, 1)
            act.wait_ge(rinv_ready, final + 1)
            for q in range(1, 2 * NB, 2):
                act.wait_ge(ot_ready, q + 1)
                nc.scalar.activation(out_rows(q), out_bank(q)[:], ACT.Copy, scale=rinv[:, q % NB:q % NB + 1]
                                     ).then_inc(ot_by_scalar, 1)

        @block.vector
        def _(dve):
            dve.sem_inc(w_ready, jobs.FIRST)
            dve.sem_inc(banks_free, jobs.FIRST)
            for d in range(DT + 3):
                if d < DT:
                    dve.wait_ge(xt_ready, d + 1)
                    nc.vector.tensor_copy(x[:, d], bank[4 + d % 4][:]).then_inc(x_ready, 1)
                if d == 3:
                    dve.wait_ge(vecs_t_ready, 1)
                    nc.vector.tensor_copy(vecs[:], bank[0][:, 0:VECS]).then_inc(vecs_ready, 1)
                    dve.wait_ge(vecs_ready, 1)
                if d >= 3:
                    gain_lo(dve, 0, d - 3)
                if d in (4, 8):
                    n = first_jobs[d // 8]
                    split_lo(dve, n, n % 2, jobs.of(n))
            for st in stages:
                if st.startswith("ffn"):
                    ffn_vector(dve, st)
                elif st.startswith("ple"):
                    ple_vector(dve, st)
                elif st.startswith("even"):
                    even_vector(dve, st)
                    rwkv_vector(dve, st)
                    out_vector(dve, st)
                elif st.startswith("fox"):
                    fox_vector(dve, st)
                    out_vector(dve, st)
            dve.wait_ge(rms_ready, final + 1)
            nc.vector.reciprocal(rinv[:, 0:NB], rms[:, 0:NB]).then_inc(rinv_ready, 1)
            dve.wait_ge(rinv_ready, final + 1)
            for q in range(0, 2 * NB, 2):
                dve.wait_ge(ot_ready, q + 1)
                nc.vector.tensor_scalar(out_rows(q), out_bank(q)[:], rinv[:, q % NB:q % NB + 1], None,
                                        ALU.mult).then_inc(ot_by_vector, 1)


def kernel(**inputs):
    import numpy as _np
    import concourse.bacc as _bacc
    from concourse import mybir as _mybir
    from concourse.bass_utils import run_bass_kernel_spmd as _run

    nc = _bacc.Bacc("TRN2", target_bir_lowering=False, num_devices=1)
    arrays, dram = {}, {}
    for name, a in inputs.items():
        arrays[f"in_{name}_dram"] = a = _np.ascontiguousarray(a)
        dram[name] = nc.dram_tensor(f"in_{name}_dram", a.shape, _mybir.dt.from_np(a.dtype),
                                    kind="ExternalInput").ap()
    out = nc.dram_tensor("out_0_dram", (1, T, DM), _mybir.dt.float32, kind="ExternalOutput").ap()
    trunk(nc, dram, out)
    r = _run(nc, [arrays], core_ids=[0])
    return r.results[0]["out_0_dram"]
```
